# Optimizing a Trainium2 kernel written in Bass

```python
import math
import jax, jax.numpy as jnp
from jax import lax
import numpy as np

D_MODEL = 1024
BATCH = 1
SEQ = 256
DEPTH = 2

N_HEADS = 8
HEAD_DIM = 64
V_HEAD_DIM = 2 * HEAD_DIM
QK_WIDTH = 2 * N_HEADS * HEAD_DIM
V_WIDTH = N_HEADS * V_HEAD_DIM
CONV_WIDTH = D_MODEL
CONV_GROUPS = 8
CONV_K = 3
SPLIT_SIZES = (QK_WIDTH, QK_WIDTH, V_WIDTH, CONV_WIDTH, CONV_WIDTH, CONV_WIDTH, D_MODEL, D_MODEL)
SPLIT_IDX = (1024, 2048, 3072, 4096, 5120, 6144, 7168)
IN_WIDTH = 8192
D_FF = 2816
N_EXPERTS = 8
TOP_K = 2
D_FF_EXPERT = 3584
N_DENSE = (DEPTH + 1) // 2
N_MOE = DEPTH // 2
ROPE_THETA = 10000.0
RMS_EPS = 1e-5
Q_BLOCK = 128

kernel_name = "hybrid_diffattn_shortconv_moe_trunk"

def rmsnorm(x, g):
    xf = x.astype(jnp.float32)
    y = xf * lax.rsqrt(jnp.mean(xf * xf, axis=-1, keepdims=True) + RMS_EPS)
    return (y * g.astype(jnp.float32)).astype(x.dtype)

def rope_tables(T, dtype):
    pos = jnp.arange(T, dtype=jnp.float32)
    inv = 1.0 / (ROPE_THETA ** (jnp.arange(0, HEAD_DIM, 2, dtype=jnp.float32) / HEAD_DIM))
    ang = pos[:, None] * inv[None, :]
    ang = jnp.concatenate([ang, ang], axis=-1)
    return jnp.cos(ang).astype(dtype), jnp.sin(ang).astype(dtype)

def apply_rope(x, cos, sin):
    x1, x2 = jnp.split(x, 2, axis=-1)
    rot = jnp.concatenate([-x2, x1], axis=-1)
    return x * cos[None, :, None, :] + rot * sin[None, :, None, :]

def diff_attention(q, k, v, lam, lam_init, subln_g):
    B, T = q.shape[0], q.shape[1]
    q = q * (HEAD_DIM ** -0.5)
    neg = jnp.finfo(jnp.float32).min
    outs = []
    for i in range(T // Q_BLOCK):
        q0 = i * Q_BLOCK
        kv_len = q0 + Q_BLOCK
        q_blk = q[:, q0:kv_len]
        k_blk = k[:, :kv_len]
        v_blk = v[:, :kv_len]
        s = jnp.einsum('bqhmd,bkhmd->bhmqk', q_blk, k_blk).astype(jnp.float32)
        q_pos = q0 + jnp.arange(Q_BLOCK)
        k_pos = jnp.arange(kv_len)
        mask = k_pos[None, :] <= q_pos[:, None]
        s = jnp.where(mask[None, None, None], s, neg)
        p = jax.nn.softmax(s, axis=-1)
        p_diff = p[:, :, 0] - lam * p[:, :, 1]
        outs.append(jnp.einsum('bhqk,bkhe->bqhe', p_diff.astype(v.dtype), v_blk))
    o = jnp.concatenate(outs, axis=1)
    o = rmsnorm(o, subln_g) * (1.0 - lam_init)
    return o.reshape(B, T, V_WIDTH)

def causal_short_conv(u, w):
    T = u.shape[1]
    up = jnp.pad(u, ((0, 0), (CONV_K - 1, 0), (0, 0)))
    y = w[0] * up[:, 0:T]
    for j in range(1, CONV_K):
        y = y + w[j] * up[:, j:j + T]
    return y

def hybrid_mixer(h, w_in, conv_w, lam_q1, lam_k1, lam_q2, lam_k2, subln_g, w_out,
                 layer_idx, cos, sin):
    B, T, _ = h.shape
    proj = h @ w_in
    q, k, v, b_g, c_g, u, g_attn, g_conv = jnp.split(proj, SPLIT_IDX, axis=-1)
    q = apply_rope(q.reshape(B, T, 2 * N_HEADS, HEAD_DIM), cos, sin)
    k = apply_rope(k.reshape(B, T, 2 * N_HEADS, HEAD_DIM), cos, sin)
    q = q.reshape(B, T, N_HEADS, 2, HEAD_DIM)
    k = k.reshape(B, T, N_HEADS, 2, HEAD_DIM)
    v = v.reshape(B, T, N_HEADS, V_HEAD_DIM)
    lam_init = 0.8 - 0.6 * math.exp(-0.3 * layer_idx)
    lam = (jnp.exp(jnp.sum(lam_q1.astype(jnp.float32) * lam_k1.astype(jnp.float32)))
           - jnp.exp(jnp.sum(lam_q2.astype(jnp.float32) * lam_k2.astype(jnp.float32)))
           + lam_init)
    y_attn = diff_attention(q, k, v, lam, lam_init, subln_g)
    y_conv = b_g * causal_short_conv(c_g * u, conv_w)
    m = jax.nn.sigmoid(g_attn) * y_attn + jax.nn.sigmoid(g_conv) * y_conv
    return m @ w_out

def swiglu(h, w_gate, w_up, w_down):
    return (jax.nn.silu(h @ w_gate) * (h @ w_up)) @ w_down

def moe_swiglu(h, w_router, e_gate, e_up, e_down):
    B, T, D = h.shape
    xt = h.reshape(B * T, D)
    logits = (xt @ w_router).astype(jnp.float32)
    top_vals, top_idx = lax.top_k(logits, TOP_K)
    top_w = jax.nn.softmax(top_vals, axis=-1)
    gates = jnp.sum(jax.nn.one_hot(top_idx, N_EXPERTS, dtype=jnp.float32) * top_w[..., None],
                    axis=1).astype(h.dtype)
    y = jnp.zeros_like(xt)
    for e in range(N_EXPERTS):
        y = y + gates[:, e:e + 1] * swiglu(xt, e_gate[e], e_up[e], e_down[e])
    return y.reshape(B, T, D)

def setup_inputs(seed: int = 0) -> dict:
    key = jax.random.key(seed)
    ks = jax.random.split(key, 24)
    f32 = jnp.float32
    nrm = lambda k, shape, scale: jax.random.normal(k, shape, f32) * scale
    return {
        "x": nrm(ks[0], (BATCH, SEQ, D_MODEL), 1.0),
        "norm_mix": 1.0 + nrm(ks[1], (DEPTH, D_MODEL), 0.02),
        "w_in": nrm(ks[2], (DEPTH, D_MODEL, IN_WIDTH), D_MODEL ** -0.5),
        "conv_w": nrm(ks[3], (DEPTH, CONV_K, CONV_WIDTH), CONV_K ** -0.5),
        "lam_q1": nrm(ks[4], (DEPTH, HEAD_DIM), 0.1),
        "lam_k1": nrm(ks[5], (DEPTH, HEAD_DIM), 0.1),
        "lam_q2": nrm(ks[6], (DEPTH, HEAD_DIM), 0.1),
        "lam_k2": nrm(ks[7], (DEPTH, HEAD_DIM), 0.1),
        "subln_g": 1.0 + nrm(ks[8], (DEPTH, V_HEAD_DIM), 0.02),
        "w_out": nrm(ks[9], (DEPTH, D_MODEL, D_MODEL), D_MODEL ** -0.5),
        "norm_ffn": 1.0 + nrm(ks[10], (DEPTH, D_MODEL), 0.02),
        "ffn_w_gate": nrm(ks[11], (N_DENSE, D_MODEL, D_FF), D_MODEL ** -0.5),
        "ffn_w_up": nrm(ks[12], (N_DENSE, D_MODEL, D_FF), D_MODEL ** -0.5),
        "ffn_w_down": nrm(ks[13], (N_DENSE, D_FF, D_MODEL), D_FF ** -0.5),
        "router_w": nrm(ks[14], (N_MOE, D_MODEL, N_EXPERTS), D_MODEL ** -0.5),
        "exp_w_gate": nrm(ks[15], (N_MOE, N_EXPERTS, D_MODEL, D_FF_EXPERT), D_MODEL ** -0.5),
        "exp_w_up": nrm(ks[16], (N_MOE, N_EXPERTS, D_MODEL, D_FF_EXPERT), D_MODEL ** -0.5),
        "exp_w_down": nrm(ks[17], (N_MOE, N_EXPERTS, D_FF_EXPERT, D_MODEL), D_FF_EXPERT ** -0.5),
        "norm_final": 1.0 + nrm(ks[18], (D_MODEL,), 0.02),
    }

def reference(x, norm_mix, w_in, conv_w, lam_q1, lam_k1, lam_q2, lam_k2, subln_g, w_out,
              norm_ffn, ffn_w_gate, ffn_w_up, ffn_w_down, router_w, exp_w_gate, exp_w_up,
              exp_w_down, norm_final):
    T = x.shape[1]
    cos, sin = rope_tables(T, x.dtype)
    for l in range(DEPTH):
        h = rmsnorm(x, norm_mix[l])
        x = x + hybrid_mixer(h, w_in[l], conv_w[l], lam_q1[l], lam_k1[l], lam_q2[l], lam_k2[l],
                             subln_g[l], w_out[l], l, cos, sin)
        h = rmsnorm(x, norm_ffn[l])
        j = l // 2
        if l % 2 == 0:
            x = x + swiglu(h, ffn_w_gate[j], ffn_w_up[j], ffn_w_down[j])
        else:
            x = x + moe_swiglu(h, router_w[j], exp_w_gate[j], exp_w_up[j], exp_w_down[j])
    return rmsnorm(x, norm_final)


_drawn_inputs = setup_inputs


def setup_inputs(seed=0):
    import zlib

    import numpy as np

    out = dict(_drawn_inputs(seed))
    spreads = {}
    factors = {}
    for name, (base, spread) in spreads.items():
        noise = np.random.default_rng([zlib.crc32(name.encode()), seed]).standard_normal(out[name].shape)
        drawn = base * np.exp(spread * noise) if base else spread * noise
        out[name] = __import__('jax').numpy.asarray(drawn.astype(out[name].dtype))
    for name, factor in factors.items():
        out[name] = (out[name] * factor).astype(out[name].dtype)
    return out
```

```python
import math
from contextlib import ExitStack

import concourse.bass as bass
from concourse import mybir

F32 = mybir.dt.float32
F32R = mybir.dt.float32r
I32 = mybir.dt.int32
ALU = mybir.AluOpType
ACT = mybir.ActivationFunctionType
AX_X = mybir.AxisListType.X

P = 128
D = 1024
T = 256
LAYERS = 2
HEADS = 8
HD = 64
VD = 2 * HD
F_DENSE = 2816
F_EXPERT = 3584
EXPERTS = 8
TAPS = 3
EPS = 1e-5
THETA = 10000.0
KD = D // P
NT = T // P
SLOTS = P
CHUNK = 512
NCH = D // CHUNK
CHUNKS_E = F_EXPERT // CHUNK
PAIRS = F_DENSE // (2 * P)

UNIT = 2048
RAW = 6
SPLIT = 4
MIX_UNITS = 4 * HEADS
OUT_UNITS = 4
FFN_UNITS = 3 * PAIRS
EXP_UNITS = 6 * CHUNKS_E
MIX0 = 0
OUT0 = MIX0 + MIX_UNITS
FFN0 = OUT0 + OUT_UNITS
MIX1 = FFN0 + FFN_UNITS
OUT1 = MIX1 + MIX_UNITS
MOE1 = OUT1 + OUT_UNITS
MOE2 = MOE1 + EXPERTS * EXP_UNITS
MIX = (MIX0, MIX1)
OUT = (OUT0, OUT1)
MOE = (MOE1, MOE2)
RAW_FIRST = {MIX0: 0, OUT0: 0, FFN0: 4, MIX1: 1, OUT1: 1, MOE1: 5, MOE2: 5}

C_ID = 0
C_COS = C_ID + P
C_SIN = C_COS + T
C_MASK = C_SIN + T
C_UPPER = C_MASK + 3 * P
C_ONES = C_UPPER + P
C_IOTA = C_ONES + P
C_TRI = C_IOTA + SLOTS
C_NH = C_TRI + EXPERTS * EXPERTS
C_EPS = C_NH + NT
C_PER_D = C_EPS + NT
C_PER_VD = C_PER_D + NT
C_ALL = C_PER_VD + NT


def lambda_init(layer):
    return 0.8 - 0.6 * math.exp(-0.3 * layer)


def unit_info(n):
    counts = [0] * RAW
    for m in range(n + 1):
        base = max(b for b in RAW_FIRST if b <= m)
        i = m - base
        four = base in (MIX0, MIX1, OUT0, OUT1)
        slot = RAW_FIRST[base] + i % 4 if four else (RAW_FIRST[base] + i) % RAW
        counts[slot] += 32 if base in MIX else 16
    return slot, (i % 4 if four else i % 3), counts[slot]


def raw_users():
    last, before = [-1] * RAW, []
    for m in range(MOE1 + RAW):
        s = unit_info(m)[0]
        before.append(last[s])
        last[s] = m
    return before


BEFORE = raw_users()


def hybrid_trunk(nc, x, w_in, w_out, gains, lam_rows, cols, router, w_gate, w_up, w_down,
                 e_gate, e_up, e_down, consts, out):
    with ExitStack() as ctx:
        def sb(name, shape, dt=F32):
            return ctx.enter_context(nc.sbuf_tensor(name, shape, dt))

        def sem(name):
            return ctx.enter_context(nc.semaphore(name))

        raw = sb("raw", [P, RAW, UNIT])
        hi = sb("hi", [P, SPLIT, UNIT], F32R)
        lo = sb("lo", [P, SPLIT, UNIT], F32R)
        xres = sb("xres", [P, NT, D])
        normed_x = sb("normed_x", [P, NT, D])
        xT_h = sb("xT_h", [P, KD * T], F32R)
        xT_l = sb("xT_l", [P, KD * T], F32R)
        mT_h = sb("mT_h", [P, KD * T], F32R)
        mT_l = sb("mT_l", [P, KD * T], F32R)
        gain = sb("gain", [P, D])
        cst = sb("cst", [P, C_ALL])
        colp = sb("colp", [P, LAYERS * KD * TAPS + LAYERS])
        sublng = sb("sublng", [P, LAYERS])
        lams = sb("lams", [P, 2, LAYERS])
        lame = sb("lame", [P, 2, LAYERS])
        lamd = sb("lamd", [P, LAYERS])
        neglam = sb("neglam", [P, LAYERS])
        ss = sb("ss", [P, NT])
        ms = sb("ms", [P, NT])
        rstd = sb("rstd", [P, NT])
        rope_s = sb("rope_s", [P, 2 * T])
        rope_c = sb("rope_c", [P, 2 * T])
        qkT = sb("qkT", [P, 2 * T])
        vb = sb("vb", [P, 2 * T])
        c_sb = sb("c_sb", [P, T])
        cu = sb("cu", [P, T + TAPS - 1])
        conv = sb("conv", [P, T])
        yconv = sb("yconv", [P, T])
        gates_t = sb("gates_t", [P, 2 * T])
        cgated = sb("cgated", [P, T])
        agated = sb("agated", [P, T])
        mix2 = sb("mix2", [P, T])
        scores = sb("scores", [P, 2, 3 * P])
        smax = sb("smax", [P, 4])
        nmax = sb("nmax", [P, 4])
        ssum = sb("ssum", [P, 4])
        srec = sb("srec", [P, 4])
        srec1 = sb("srec1", [P, 2])
        pm1 = sb("pm1", [P, 3 * P])
        pdiff = sb("pdiff", [P, 3 * P])
        pT = sb("pT", [P, 3 * P])
        osq = sb("osq", [P, NT])
        oms = sb("oms", [P, NT])
        orstd = sb("orstd", [P, NT])
        onorm = sb("onorm", [P, T])
        hT_h = sb("hT_h", [P, CHUNK], F32R)
        hT_l = sb("hT_l", [P, CHUNK], F32R)
        rw = sb("rw", [P, KD * EXPERTS])
        rw_h = sb("rw_h", [P, KD * EXPERTS], F32R)
        rw_l = sb("rw_l", [P, KD * EXPERTS], F32R)
        logit = sb("logit", [P, NT, EXPERTS])
        above = sb("above", [P, NT, EXPERTS, EXPERTS])
        ties = sb("ties", [P, NT, EXPERTS, EXPERTS])
        rank = sb("rank", [P, NT, EXPERTS])
        top1 = sb("top1", [P, NT, EXPERTS])
        top2 = sb("top2", [P, NT, EXPERTS])
        v1 = sb("v1", [P, NT])
        v2 = sb("v2", [P, NT])
        v2e = sb("v2e", [P, NT])
        den = sb("den", [P, NT])
        w1 = sb("w1", [P, NT])
        w2 = sb("w2", [P, NT])
        chosen = sb("chosen", [P, NT, EXPERTS])
        egate = sb("egate", [P, NT, EXPERTS])
        place = sb("place", [P, NT, EXPERTS])
        most = sb("most", [P, 1])
        most_i = sb("most_i", [P, 1], I32)
        pick = sb("pick", [P, NT, SLOTS], F32R)
        pickT = sb("pickT", [P, T], F32R)
        mark = sb("mark", [P, 1])

        bank = ctx.enter_context(nc.psum_tensor("bank", [P, 8, CHUNK], F32))

        landed = [sem(f"landed{i}") for i in range(RAW)]
        s_small = sem("s_small")
        s_gain = sem("s_gain")
        s_hi = sem("s_hi")
        s_lo = sem("s_lo")
        s_pe = sem("s_pe")
        s_setup = sem("s_setup")
        s_setup_a = sem("s_setup_a")
        s_setup_p = sem("s_setup_p")
        s_ss = sem("s_ss")
        s_ms = sem("s_ms")
        s_rstd = sem("s_rstd")
        s_normed = sem("s_normed")
        s_turned = sem("s_turned")
        s_xt_h = sem("s_xt_h")
        s_xt = sem("s_xt")
        s_xres = sem("s_xres")
        s_rope1 = sem("s_rope1")
        s_roped = sem("s_roped")
        s_scores = sem("s_scores")
        s_masked = sem("s_masked")
        s_maxed = sem("s_maxed")
        s_nmax = sem("s_nmax")
        s_exp = sem("s_exp")
        s_srec = sem("s_srec")
        s_srec1 = sem("s_srec1")
        s_pm1 = sem("s_pm1")
        s_pdiff = sem("s_pdiff")
        s_pturn = sem("s_pturn")
        s_pT = sem("s_pT")
        s_vb = sem("s_vb")
        s_pv = sem("s_pv")
        s_osq = sem("s_osq")
        s_oms = sem("s_oms")
        s_orstd = sem("s_orstd")
        s_onorm = sem("s_onorm")
        s_oturn = sem("s_oturn")
        s_c = sem("s_c")
        s_cu = sem("s_cu")
        s_tap = sem("s_tap")
        s_conv = sem("s_conv")
        s_gates = sem("s_gates")
        s_agated = sem("s_agated")
        s_mix2 = sem("s_mix2")
        s_cgated = sem("s_cgated")
        s_mT_h = sem("s_mT_h")
        s_mT = sem("s_mT")
        s_fsilu = sem("s_fsilu")
        s_fhid = sem("s_fhid")
        s_fhT_h = sem("s_fhT_h")
        s_fhT = sem("s_fhT")
        s_rw_h = sem("s_rw_h")
        s_rw = sem("s_rw")
        s_nx_h = sem("s_nx_h")
        s_nx = sem("s_nx")
        s_logit = sem("s_logit")
        s_route = sem("s_route")
        s_v2e = sem("s_v2e")
        s_chosen = sem("s_chosen")
        s_count = sem("s_count")
        s_most = sem("s_most")
        s_esilu = sem("s_esilu")
        s_ehid = sem("s_ehid")
        s_ehturn = sem("s_ehturn")
        s_ehT_h = sem("s_ehT_h")
        s_ehT = sem("s_ehT")
        s_pick = sem("s_pick")
        s_pick_s = sem("s_pick_s")
        s_gather = sem("s_gather")
        s_xg_h = sem("s_xg_h")
        s_xg = sem("s_xg")
        s_pickturn = sem("s_pickturn")
        s_pickT = sem("s_pickT")
        s_eo_h = sem("s_eo_h")
        s_eo = sem("s_eo")
        s_scatter = sem("s_scatter")
        s_combined = sem("s_combined")
        s_stored = sem("s_stored")

        ident = cst[:, C_ID:C_ID + P]
        xTh = xT_h[:].rearrange("p (k t) -> p k t", k=KD)
        xTl = xT_l[:].rearrange("p (k t) -> p k t", k=KD)
        mTh = mT_h[:].rearrange("p (k t) -> p k t", k=KD)
        mTl = mT_l[:].rearrange("p (k t) -> p k t", k=KD)
        nxh = mT_h[:].rearrange("p (t d) -> p t d", t=NT)
        nxl = mT_l[:].rearrange("p (t d) -> p t d", t=NT)
        xgh = xT_h[:, 0:KD * SLOTS].rearrange("p (k s) -> p k s", k=KD)
        xgl = xT_l[:, 0:KD * SLOTS].rearrange("p (k s) -> p k s", k=KD)

        lamv = scores[:].rearrange("p m n -> p (m n)")[:, 0:4 * LAYERS * HD].rearrange(
            "p (a l d) -> p a l d", a=4, l=LAYERS)
        lamp = pdiff[:, 0:2 * LAYERS * HD].rearrange("p (a l d) -> p a l d", a=2, l=LAYERS)
        silu_g, hid = rope_s, rope_c
        pick_s = gates_t[:, 0:NT * SLOTS].rearrange("p (t s) -> p t s", t=NT)
        eo_h = xT_h[:, KD * SLOTS:KD * SLOTS + D]
        eo_l = xT_l[:, KD * SLOTS:KD * SLOTS + D]

        def block_of(buf, slot, **sizes):
            pattern = "p (" + " ".join(sizes) + " n) -> p " + " ".join(sizes) + " n"
            return buf[:, slot, :].rearrange(pattern, **sizes)

        block = ctx.enter_context(nc.Block())

        @block.sync
        def _(sp):
            w_in_v = [w_in[l].rearrange("(k p) n -> p k n", p=P) for l in range(LAYERS)]
            w_out_v = [w_out[l].rearrange("(k p) n -> p k n", p=P) for l in range(LAYERS)]
            gate_v = w_gate.rearrange("a (k p) f -> p (a k) f", p=P)
            up_v = w_up.rearrange("a (k p) f -> p (a k) f", p=P)
            down_v = w_down.rearrange("a (r p) n -> p (a r) n", p=P)
            egate_v = e_gate.rearrange("a e (k p) f -> p (a e k) f", p=P)
            eup_v = e_up.rearrange("a e (k p) f -> p (a e k) f", p=P)
            edown_v = e_down.rearrange("a e (r p) n -> p (a e r) n", p=P)

            def load_gain(q):
                if q:
                    sp.wait_ge(s_normed, NT * q)
                sp.dma_start(gain[:], gains[q:q + 1, :].to_broadcast([P, D])).then_inc(s_gain, 16)

            def load_mixer(l, j, u, slot):
                for s in range(2):
                    part = raw[:, slot, s * (UNIT // 2):(s + 1) * (UNIT // 2)].rearrange("p (k c) -> p k c", k=KD)
                    sp.dma_start(part, w_in_v[l][:, :, bass.ds((2 * u + s) * D + j * P, P)]).then_inc(landed[slot], 16)

            def mixer_loads(l):
                for u in range(4):
                    before = BEFORE[MIX[l] + u]
                    if before >= 0:
                        sp.wait_ge(s_lo, before + 1)
                    load_mixer(l, 0, u, RAW_FIRST[MIX[l]] + u)
                with sp.Fori(1, HEADS) as j:
                    for u in range(4):
                        sp.wait_ge(s_lo, MIX[l] + 4 * j + u - 3)
                        load_mixer(l, j, u, RAW_FIRST[MIX[l]] + u)

            def out_loads(l):
                for u in range(OUT_UNITS):
                    slot = unit_info(OUT[l] + u)[0]
                    sp.wait_ge(s_lo, BEFORE[OUT[l] + u] + 1)
                    sp.dma_start(block_of(raw, slot, k=2), w_out_v[l][:, 2 * u:2 * u + 2, :]).then_inc(landed[slot], 16)

            def ffn_load(kind, i, n, slot):
                if kind == "d":
                    dst, src = block_of(raw, slot, r=2), down_v[:, bass.ds(2 * i, 2), :]
                else:
                    dst, src = block_of(raw, slot, k=KD), (gate_v if kind == "g" else up_v)[:, :, bass.ds(i * 2 * P, 2 * P)]
                sp.dma_start(dst, src).then_inc(landed[slot], 16)

            def ffn_loads():
                first = [("g", 0), ("u", 0), ("g", 1), ("u", 1), ("d", 0), ("g", 2), ("u", 2), ("d", 1)]
                for n, (kind, i) in enumerate(first):
                    before = BEFORE[FFN0 + n]
                    if before >= 0:
                        sp.wait_ge(s_lo, before + 1)
                    ffn_load(kind, i, n, unit_info(FFN0 + n)[0])
                with sp.Fori(0, (PAIRS - 3) // 2) as r:
                    for m in range(6):
                        n = len(first) + m
                        sp.wait_ge(s_lo, FFN0 + n - RAW + 1 + 6 * r)
                        i = 3 + m // 3
                        ffn_load("gud"[m % 3], 2 * r + (i if m % 3 < 2 else i - 1), n, unit_info(FFN0 + n)[0])
                n = FFN_UNITS - 1
                sp.wait_ge(s_lo, FFN0 + n - RAW + 1)
                ffn_load("d", PAIRS - 1, n, unit_info(FFN0 + n)[0])

            def expert_chunk(base, e, c, kinds, at):
                for m, kind in enumerate(kinds):
                    half = m % 2
                    slot = (5 + at + m) % RAW
                    sp.wait_ge(s_lo, base + m - RAW + 1)
                    if kind == "d":
                        src = edown_v[:, bass.ds(e * (F_EXPERT // P) + 4 * (c - 1) + 2 * half, 2), :]
                        dst = block_of(raw, slot, r=2)
                    else:
                        v = egate_v if kind == "g" else eup_v
                        src = v[:, bass.ds(e * KD + 4 * half, 4), bass.ds(c * CHUNK, CHUNK)]
                        dst = block_of(raw, slot, k=4)
                    sp.dma_start(dst, src).then_inc(landed[slot], 16)

            def expert_loads(start):
                with sp.Fori(0, EXPERTS) as e:
                    n0 = start + EXP_UNITS * e
                    expert_chunk(n0, e, 0, "gguu", 0)
                    with sp.Fori(1, CHUNKS_E) as c:
                        expert_chunk(n0 + 4 + 6 * (c - 1), e, c, "gguudd", 4)
                    expert_chunk(n0 + EXP_UNITS - 2, e, CHUNKS_E, "dd", 4)

            sp.dma_start(xres[:], x.rearrange("(t p) d -> p t d", p=P)).then_inc(s_small, 16)
            sp.dma_start(cst[:], consts).then_inc(s_small, 16)
            sp.dma_start(colp[:], cols).then_inc(s_small, 16)
            sp.dma_start(rw[:], router).then_inc(s_small, 16)
            sp.dma_start(lamv.rearrange("p a l d -> p (a l d)"),
                         lam_rows.to_broadcast([P, 4 * LAYERS * HD])).then_inc(s_small, 16)
            load_gain(0)
            mixer_loads(0)
            load_gain(1)
            out_loads(0)
            ffn_loads()
            load_gain(2)
            mixer_loads(1)
            load_gain(3)
            out_loads(1)
            expert_loads(MOE1)
            load_gain(4)
            sp.wait_ge(s_most, 2)
            with sp.If(sp.value_load(most_i[0:1, 0:1], min_val=0, max_val=T) > SLOTS):
                expert_loads(MOE2)
            sp.wait_ge(s_normed, NT * 5)
            sp.dma_start(out.rearrange("(t p) d -> p t d", p=P), normed_x[:]).then_inc(s_stored, 16)
            sp.wait_ge(s_stored, 16)

        def splits_after(split, phase_end_of):
            for n in phase_end_of:
                split(n)

        @block.scalar
        def _(act):
            def copy(dst, src, s, scale=1.0):
                nc.scalar.activation(dst, src, ACT.Copy, scale=scale).then_inc(s, 1)

            def split(slot, part, count, used):
                act.wait_ge(landed[slot], count)
                if used is not None:
                    act.wait_ge(s_pe, used)
                copy(hi[:, part, :], raw[:, slot, :], s_hi)

            def split_unit(n, used):
                slot, part, count = unit_info(n)
                split(slot, part, count, used)

            def norm(q):
                if q == 0:
                    act.wait_ge(s_small, 5 * 16)
                else:
                    act.wait_ge(s_xres, q)
                for t in range(NT):
                    last = nc.scalar.activation(normed_x[:, t, :], xres[:, t, :], ACT.Square, accum_out=ss[:, t:t + 1])
                last.then_inc(s_ss, 1)
                if q == 4:
                    return
                if q == 3:
                    for t in range(NT):
                        act.wait_ge(s_normed, NT * q + t + 1)
                        copy(nxh[:, t, :], normed_x[:, t, :], s_nx_h)
                for b in range(4):
                    t, half = b // 2, b % 2
                    act.wait_ge(s_turned, 4 * q + b + 1)
                    copy(xTh[:, 4 * half:4 * half + 4, t * P:(t + 1) * P],
                         bank[:, 4 + b, :].rearrange("p (k t) -> p k t", k=4), s_xt_h)

            def attention_a(J):
                act.wait_ge(s_pturn, J)
                copy(pT[:], bank[:, 6, 0:3 * P], s_pT)

            def attention_b(J):
                act.wait_ge(s_pv, J)
                for t in range(NT):
                    last = nc.scalar.activation(onorm[:, t * P:(t + 1) * P], bank[:, 7, t * P:(t + 1) * P],
                                                ACT.Square, accum_out=osq[:, t:t + 1])
                last.then_inc(s_osq, 1)

            def attention_c(J, j):
                act.wait_ge(s_mix2, J)
                copy(mTh[:, bass.ds(j, 1), :], mix2[:].rearrange("p (a t) -> p a t", a=1), s_mT_h, scale=0.5)

            def head(l, j, next_units):
                J = HEADS * l + j
                first = isinstance(j, int) and j == 0
                never = first and l == 0
                n = MIX[l] + 4 * j
                next_units(0)
                if not first:
                    attention_a(J)
                next_units(1)
                if not never:
                    act.wait_ge(s_pv, J)
                    act.wait_ge(s_conv, J)
                act.wait_ge(s_pe, n + 2)
                copy(vb[:], bank[:, 1, :], s_vb)
                if not first:
                    attention_b(J)
                next_units(2)
                act.wait_ge(s_pe, n + 3)
                copy(c_sb[:], bank[:, 2, 0:T], s_c)
                act.wait_ge(s_nmax, J + 1)
                for i in range(NT):
                    lo_k, hi_k = (0, P) if i == 0 else (P, 3 * P)
                    for m in range(2):
                        s = scores[:, m, lo_k:hi_k]
                        last = nc.scalar.activation(s, s, ACT.Exp, bias=nmax[:, 2 * i + m:2 * i + m + 1],
                                                    scale=HD ** -0.5, accum_out=ssum[:, 2 * i + m:2 * i + m + 1])
                last.then_inc(s_exp, 1)
                next_units(3)
                if not never:
                    act.wait_ge(s_mix2, J)
                act.wait_ge(s_pe, n + 4)
                nc.scalar.activation(gates_t[:], bank[:, 3, :], ACT.Tanh, scale=0.5).then_inc(s_gates, 1)
                if not first:
                    attention_c(J, j - 1)

            def mixer(l):
                head(l, 0, lambda u: split_unit(MIX[l] + 4 + u, MIX[l] + u + 1))
                base = [unit_info(MIX[l] + 4 + u)[2] for u in range(4)]

                def loop(j):
                    def nxt(u):
                        slot = RAW_FIRST[MIX[l]] + u
                        split(slot, u, base[u] + 32 * j, MIX[l] + 4 * j + u + 1)
                    head(l, j, nxt)
                with act.Fori(1, HEADS - 1) as j:
                    loop(j)
                head(l, HEADS - 1, lambda u: split_unit(OUT[l] + u, MIX[l] + 4 * (HEADS - 1) + u + 1))
                J = HEADS * (l + 1)
                attention_a(J)
                attention_b(J)
                attention_c(J, HEADS - 1)

            def ffn_silu(i, n):
                if not (isinstance(i, int) and i == 0):
                    act.wait_ge(s_fhid, i)
                act.wait_ge(s_pe, n + 1)
                nc.scalar.activation(silu_g[:], bank[:, 4, :], ACT.Silu).then_inc(s_fsilu, 1)

            def ffn_hT(i):
                act.wait_ge(s_fhid, i + 1)
                copy(hT_h[:], hid[:], s_fhT_h)

            def ffn():
                n = FFN0
                split_unit(n + 3, n + 1)
                ffn_silu(0, n)
                split_unit(n + 4, n + 2)
                ffn_hT(0)
                for i in (1, 2):
                    n = FFN0 + 3 * i - 1
                    split_unit(n + 3, n + 1)
                    ffn_silu(i, n)
                    split_unit(n + 4, n + 2)
                    split_unit(n + 5, n + 3)
                    ffn_hT(i)
                counts = [unit_info(FFN0 + 8 + m + 3)[2] for m in range(6)]
                with act.Fori(0, (PAIRS - 3) // 2 - 1) as r:
                    for m in range(6):
                        i = 3 + m // 3 + 2 * r
                        n = FFN0 + 8 + m
                        slot, part, _ = unit_info(n + 3)
                        split(slot, part, counts[m] + 16 * r, n + 1 + 6 * r)
                        if m % 3 == 0:
                            ffn_silu(i, n + 6 * r)
                        if m % 3 == 2:
                            ffn_hT(i)
                for i in (PAIRS - 2, PAIRS - 1):
                    n = FFN0 + 3 * i - 1
                    split_unit(n + 3, n + 1)
                    ffn_silu(i, n)
                    if n + 4 < FFN0 + FFN_UNITS:
                        split_unit(n + 4, n + 2)
                        split_unit(n + 5, n + 3)
                    else:
                        split_unit(MIX1, FFN0 + 31)
                        split_unit(MIX1 + 1, FFN0 + 32)
                    ffn_hT(i)
                split_unit(MIX1 + 2, FFN0 + 33)
                split_unit(MIX1 + 3, FFN0 + 33)

            def expert_chunk(C, n, at, counts, with_down, skip=0):
                for m in range(6 if with_down else 4):
                    if m < 6 - skip:
                        split((5 + at + m + 3) % RAW, (at + m) % 3, counts(m), n + m + 1)
                    if m == 1:
                        if not (isinstance(C, int) and C == 0):
                            act.wait_ge(s_ehid, C)
                        nc.scalar.activation(silu_g[:], bank[:, 2, :], ACT.Silu).then_inc(s_esilu, 1)
                act.wait_ge(s_ehturn, C + 1)
                copy(hT_h[:], bank[:, 4, :], s_ehT_h)

            def gathered(E):
                act.wait_ge(s_gather, E + 1)
                copy(xT_h[:, 0:D].rearrange("p (b n) -> p b n", b=2), bank[:, 5:7, :], s_xg_h)

            def expert(pas, e, last):
                E = EXPERTS * pas + e
                C = CHUNKS_E * E
                n = MOE[pas] + EXP_UNITS * e
                base = [unit_info(MOE[pas] + 3 + m)[2] for m in range(RAW)]

                def counts(i, c):
                    return base[i % 6] + 16 * (CHUNKS_E * e + c + i // 6)
                expert_chunk(C, n, 0, lambda m: counts(m, 0), False)
                expert_chunk(C + 1, n + 4, 4, lambda m: counts(4 + m, 0), True)
                with act.Fori(2, CHUNKS_E - 1 if last else CHUNKS_E) as c:
                    expert_chunk(C + c, n + 4 + 6 * (c - 1), 4, lambda m: counts(4 + m, c - 1), True)
                if last:
                    expert_chunk(C + CHUNKS_E - 1, n + EXP_UNITS - 8, 4, lambda m: counts(4 + m, CHUNKS_E - 2),
                                 True, skip=1)
                act.wait_ge(s_pickturn, E + 1)
                copy(pickT[:], bank[:, 7, 0:T], s_pickT)
                if not last:
                    gathered(E + 1)
                    for m in range(EXP_UNITS - 2, EXP_UNITS):
                        split((5 + m + 3) % RAW, m % 3, counts(m, 0), n + m + 1)
                if not (isinstance(E, int) and E == 0):
                    act.wait_ge(s_scatter, E)
                act.wait_ge(s_pe, n + EXP_UNITS)
                copy(eo_h.rearrange("p (b n) -> p b n", b=2), bank[:, 0:2, :], s_eo_h)

            def experts(pas):
                gathered(EXPERTS * pas)
                expert(pas, 0, False)
                with act.Fori(1, EXPERTS - 1) as e:
                    expert(pas, e, False)
                expert(pas, EXPERTS - 1, True)

            act.wait_ge(s_setup, 2)
            nc.scalar.activation(lame[:], lams[:], ACT.Exp).then_inc(s_setup_a, 1)
            norm(0)
            for n in range(4):
                split_unit(n, None)
            mixer(0)
            for n in range(3):
                split_unit(FFN0 + n, OUT0 + n + 1)
            norm(1)
            ffn()
            norm(2)
            mixer(1)
            for n in range(3):
                split_unit(MOE1 + n, OUT1 + n + 1)
            copy(rw_h[:], rw[:], s_rw_h)
            norm(3)
            act.wait_ge(s_route, 6)
            nc.scalar.activation(v2e[:], v2[:], ACT.Exp).then_inc(s_v2e, 1)
            experts(0)
            act.wait_ge(s_most, 2)
            with act.If(act.value_load(most_i[0:1, 0:1], min_val=0, max_val=T) > SLOTS):
                for n in range(3):
                    split_unit(MOE2 + n, MOE2)
                experts(1)
            norm(4)

        @block.vector
        def _(dve):
            v = nc.vector
            steps = [0]

            def step(ins):
                ins.then_inc(s_setup, 1)
                steps[0] += 1
                dve.wait_ge(s_setup, steps[0])

            def split(n, slot, part):
                dve.wait_ge(s_hi, n + 1)
                v.tensor_tensor(lo[:, part, :], raw[:, slot, :], hi[:, part, :].bitcast(F32),
                                ALU.subtract).then_inc(s_lo, 1)

            def split_unit(n):
                slot, part, _ = unit_info(n)
                split(n, slot, part)

            def norm(q):
                dve.wait_ge(s_gain, 16 * (q + 1))
                dve.wait_ge(s_rstd, q + 1)
                for t in range(NT):
                    v.scalar_tensor_tensor(out=normed_x[:, t, :], in0=xres[:, t, :], scalar=rstd[:, t:t + 1],
                                           in1=gain[:], op0=ALU.mult, op1=ALU.mult).then_inc(s_normed, 1)
                if q == 4:
                    return
                if q == 3:
                    for t in range(NT):
                        dve.wait_ge(s_nx_h, t + 1)
                        v.tensor_tensor(nxl[:, t, :], normed_x[:, t, :], nxh[:, t, :].bitcast(F32),
                                        ALU.subtract).then_inc(s_nx, 1)
                for b in range(4):
                    t, half = b // 2, b % 2
                    dve.wait_ge(s_xt_h, 4 * q + b + 1)
                    dst = xTl[:, 4 * half:4 * half + 4, t * P:(t + 1) * P]
                    top = xTh[:, 4 * half:4 * half + 4, t * P:(t + 1) * P].bitcast(F32)
                    v.tensor_tensor(dst, bank[:, 4 + b, :].rearrange("p (k t) -> p k t", k=4), top,
                                    ALU.subtract).then_inc(s_xt, 1)

            def rope(J, n):
                dve.wait_ge(s_pe, n + 1)
                if not (isinstance(J, int) and J == 0):
                    dve.wait_ge(s_scores, J)
                both = bank[:, 0, :].rearrange("p (s t) -> p s t", s=2)
                sines, cosines = (cst[:, c:c + T].unsqueeze(1).to_broadcast([P, 2, T]) for c in (C_SIN, C_COS))
                rs, rc = (b[:].rearrange("p (s t) -> p s t", s=2) for b in (rope_s, rope_c))
                for q in range(4):
                    src, dst = slice(32 * q, 32 * q + 32), slice(32 * (q ^ 1), 32 * (q ^ 1) + 32)
                    v.tensor_tensor(rs[dst], both[src], sines[src], ALU.mult)
                v.tensor_tensor(rc, both, cosines, ALU.mult).then_inc(s_rope1, 1)
                dve.wait_ge(s_rope1, J + 1)
                v.tensor_tensor(qkT[:], rope_s[:], rope_c[:], ALU.add).then_inc(s_roped, 1)

            def attention_b(J):
                dve.wait_ge(s_orstd, J)
                for t in range(NT):
                    last = v.tensor_scalar(onorm[:, t * P:(t + 1) * P], bank[:, 7, t * P:(t + 1) * P],
                                           orstd[:, t:t + 1], None, ALU.mult)
                last.then_inc(s_onorm, 1)

            def attention_c1(l, J):
                dve.wait_ge(s_oturn, J)
                dve.wait_ge(s_gates, J)
                v.scalar_tensor_tensor(out=agated[:], in0=gates_t[:, 0:T], scalar=1.0, in1=bank[:, 7, T:2 * T],
                                       op0=ALU.add, op1=ALU.mult).then_inc(s_agated, 1)
                dve.wait_ge(s_agated, J)
                dve.wait_ge(s_cgated, J)
                v.scalar_tensor_tensor(out=mix2[:], in0=agated[:], scalar=sublng[:, l:l + 1], in1=cgated[:],
                                       op0=ALU.mult, op1=ALU.add).then_inc(s_mix2, 1)

            def attention_c2(J, j):
                dve.wait_ge(s_mT_h, J)
                v.scalar_tensor_tensor(out=mTl[:, bass.ds(j, 1), :], in0=mix2[:].rearrange("p (a t) -> p a t", a=1),
                                       scalar=0.5, in1=mTh[:, bass.ds(j, 1), :].bitcast(F32),
                                       op0=ALU.mult, op1=ALU.subtract).then_inc(s_mT, 1)

            def softmax_max(J):
                dve.wait_ge(s_scores, J + 1)
                for m in range(2):
                    last = v.tensor_tensor(scores[:, m, :], bank[:, 4 + m, 0:3 * P], cst[:, C_MASK:C_MASK + 3 * P], ALU.add)
                last.then_inc(s_masked, 1)
                dve.wait_ge(s_masked, J + 1)
                v.tensor_reduce(smax[:, 0:2], scores[:, :, 0:P], AX_X, ALU.max)
                v.tensor_reduce(smax[:, 2:4], scores[:, :, P:3 * P], AX_X, ALU.max).then_inc(s_maxed, 1)
                dve.wait_ge(s_maxed, J + 1)
                v.tensor_scalar(nmax[:], smax[:], -HD ** -0.5, None, ALU.mult).then_inc(s_nmax, 1)

            def short_conv(l, J, j):
                dve.wait_ge(s_c, J + 1)
                v.tensor_tensor(cu[:, TAPS - 1:], bank[:, 2, T:2 * T], c_sb[:], ALU.mult).then_inc(s_cu, 1)
                dve.wait_ge(s_cu, J + 1)
                tap = [colp[:, bass.ds(TAPS * (KD * l + j) + i, 1)] for i in range(TAPS)]
                v.tensor_scalar(conv[:], cu[:, 0:T], tap[0], None, ALU.mult).then_inc(s_tap, 1)
                for i in range(1, TAPS):
                    dve.wait_ge(s_tap, TAPS * J + i)
                    v.scalar_tensor_tensor(out=conv[:], in0=cu[:, i:i + T], scalar=tap[i], in1=conv[:],
                                           op0=ALU.mult, op1=ALU.add).then_inc(s_tap, 1)
                dve.wait_ge(s_tap, TAPS * (J + 1))
                dve.wait_ge(s_vb, J + 1)
                v.tensor_tensor(yconv[:], conv[:], vb[:, T:2 * T], ALU.mult).then_inc(s_conv, 1)

            def gate_conv(J):
                dve.wait_ge(s_gates, J + 1)
                dve.wait_ge(s_conv, J + 1)
                v.scalar_tensor_tensor(out=cgated[:], in0=gates_t[:, T:2 * T], scalar=1.0, in1=yconv[:],
                                       op0=ALU.add, op1=ALU.mult).then_inc(s_cgated, 1)

            def prob_diff(l, J):
                dve.wait_ge(s_exp, J + 1)
                v.reciprocal(srec[:], ssum[:]).then_inc(s_srec, 1)
                dve.wait_ge(s_srec, J + 1)
                v.tensor_scalar(srec1[:], srec[:].rearrange("p (i m) -> p i m", m=2)[:, :, 1], neglam[:, l:l + 1],
                                None, ALU.mult).then_inc(s_srec1, 1)
                dve.wait_ge(s_srec1, J + 1)
                spans = [(0, P), (P, 3 * P)]
                for i, (a, b) in enumerate(spans):
                    last = v.tensor_scalar(pm1[:, a:b], scores[:, 1, a:b], srec1[:, i:i + 1], None, ALU.mult)
                last.then_inc(s_pm1, 1)
                dve.wait_ge(s_pm1, J + 1)
                for i, (a, b) in enumerate(spans):
                    last = v.scalar_tensor_tensor(out=pdiff[:, a:b], in0=scores[:, 0, a:b],
                                                  scalar=srec[:, 2 * i:2 * i + 1], in1=pm1[:, a:b],
                                                  op0=ALU.mult, op1=ALU.add)
                last.then_inc(s_pdiff, 1)

            def head(l, j, next_units):
                J = HEADS * l + j
                first = isinstance(j, int) and j == 0
                n = MIX[l] + 4 * j
                next_units(0)
                rope(J, n)
                next_units(1)
                if not first:
                    attention_b(J)
                next_units(2)
                softmax_max(J)
                short_conv(l, J, j)
                next_units(3)
                if not first:
                    attention_c1(l, J)
                gate_conv(J)
                if not first:
                    attention_c2(J, j - 1)
                prob_diff(l, J)

            def mixer(l):
                head(l, 0, lambda u: split_unit(MIX[l] + 4 + u))
                with dve.Fori(1, HEADS - 1) as j:
                    head(l, j, lambda u: split(MIX[l] + 4 * j + 4 + u, RAW_FIRST[MIX[l]] + u, u))
                head(l, HEADS - 1, lambda u: split_unit(OUT[l] + u))
                J = HEADS * (l + 1)
                attention_b(J)
                attention_c1(l, J)
                attention_c2(J, HEADS - 1)

            def residual(unit):
                dve.wait_ge(s_pe, unit + 1)
                for b in range(4):
                    part = xres[:, b // 2, (b % 2) * CHUNK:(b % 2 + 1) * CHUNK]
                    last = v.tensor_tensor(part, bank[:, b, :], part, ALU.add)
                last.then_inc(s_xres, 1)

            def ffn_hid(i, n):
                if not (isinstance(i, int) and i == 0):
                    dve.wait_ge(s_fhT, i)
                dve.wait_ge(s_fsilu, i + 1)
                dve.wait_ge(s_pe, n + 1)
                v.tensor_tensor(hid[:], bank[:, 5, :], silu_g[:], ALU.mult).then_inc(s_fhid, 1)

            def ffn_hT(i):
                dve.wait_ge(s_fhT_h, i + 1)
                v.tensor_tensor(hT_l[:], hid[:], hT_h[:].bitcast(F32), ALU.subtract).then_inc(s_fhT, 1)

            def ffn():
                split_unit(FFN0 + 3)
                split_unit(FFN0 + 4)
                ffn_hid(0, FFN0 + 1)
                ffn_hT(0)
                for i in (1, 2):
                    n = FFN0 + 3 * i - 1
                    split_unit(n + 3)
                    split_unit(n + 4)
                    ffn_hid(i, n + 1)
                    split_unit(n + 5)
                    ffn_hT(i)
                with dve.Fori(0, (PAIRS - 3) // 2 - 1) as r:
                    for m in range(6):
                        i = 3 + m // 3 + 2 * r
                        n = FFN0 + 8 + m
                        slot, part, _ = unit_info(n + 3)
                        split(n + 3 + 6 * r, slot, part)
                        if m % 3 == 1:
                            ffn_hid(i, n + 6 * r)
                        if m % 3 == 2:
                            ffn_hT(i)
                for i in (PAIRS - 2, PAIRS - 1):
                    n = FFN0 + 3 * i - 1
                    split_unit(n + 3)
                    split_unit(n + 4 if i == PAIRS - 2 else MIX1)
                    ffn_hid(i, n + 1)
                    split_unit(n + 5 if i == PAIRS - 2 else MIX1 + 1)
                    ffn_hT(i)
                split_unit(MIX1 + 2)
                split_unit(MIX1 + 3)

            def route():
                dve.wait_ge(s_rw_h, 1)
                v.tensor_tensor(rw_l[:], rw[:], rw_h[:].bitcast(F32), ALU.subtract).then_inc(s_rw, 1)

            r_steps = [0]

            def rstep(ins):
                ins.then_inc(s_route, 1)
                r_steps[0] += 1
                dve.wait_ge(s_route, r_steps[0])

            def top_two():
                dve.wait_ge(s_logit, 1)
                rstep(v.tensor_copy(logit[:], bank[:, 0, 0:NT * EXPERTS].rearrange("p (t e) -> p t e", t=NT)))
                mine = logit[:].unsqueeze(3).to_broadcast([P, NT, EXPERTS, EXPERTS])
                other = logit[:].unsqueeze(2).to_broadcast([P, NT, EXPERTS, EXPERTS])
                tri = cst[:, C_TRI:C_TRI + EXPERTS * EXPERTS].rearrange("p (e j) -> p e j", e=EXPERTS)
                v.tensor_tensor(above[:], other, mine, ALU.is_gt)
                rstep(v.tensor_tensor(ties[:], other, mine, ALU.is_equal))
                for t in range(NT):
                    last = v.tensor_tensor(ties[:, t], ties[:, t], tri, ALU.mult)
                rstep(last)
                rstep(v.tensor_tensor(above[:], above[:], ties[:], ALU.add))
                v.tensor_reduce(rank[:], above[:], AX_X, ALU.add)
                rstep(v.tensor_reduce(v1[:], logit[:], AX_X, ALU.max))
                v.tensor_scalar(top1[:], rank[:], 0.0, None, ALU.is_equal)
                v.tensor_scalar(chosen[:], rank[:], 2.0, None, ALU.is_lt)
                v.tensor_scalar(top2[:], rank[:], 1.0, None, ALU.is_equal).then_inc(s_chosen, 1)
                dve.wait_ge(s_chosen, 1)
                v.tensor_tensor(ties[:, :, 0, :], top2[:], logit[:], ALU.mult).then_inc(s_chosen, 1)
                dve.wait_ge(s_chosen, 2)
                v.tensor_reduce(w2[:], ties[:, :, 0, :], AX_X, ALU.add).then_inc(s_chosen, 1)
                dve.wait_ge(s_chosen, 3)
                rstep(v.tensor_tensor(v2[:], w2[:], v1[:], ALU.subtract))
                dve.wait_ge(s_v2e, 1)
                rstep(v.tensor_scalar(den[:], v2e[:], 1.0, None, ALU.add))
                rstep(v.reciprocal(w1[:], den[:]))
                rstep(v.tensor_tensor(w2[:], w1[:], v2e[:], ALU.mult))
                for t in range(NT):
                    last = v.tensor_scalar(egate[:, t, :], top1[:, t, :], w1[:, t:t + 1], None, ALU.mult)
                rstep(last)
                for t in range(NT):
                    last = v.scalar_tensor_tensor(out=egate[:, t, :], in0=top2[:, t, :], scalar=w2[:, t:t + 1],
                                                  in1=egate[:, t, :], op0=ALU.mult, op1=ALU.add)
                rstep(last)
                dve.wait_ge(s_count, 1)
                rstep(v.tensor_scalar(place[:], bank[:, 1, 0:NT * EXPERTS].rearrange("p (t e) -> p t e", t=NT),
                                      1.0, None, ALU.add))
                rstep(v.tensor_tensor(place[:], place[:], chosen[:], ALU.mult))
                rstep(v.tensor_scalar(place[:], place[:], -1.0, None, ALU.add))
                v.tensor_reduce(most[:], bank[:, 1, NT * EXPERTS:(NT + 1) * EXPERTS], AX_X, ALU.max).then_inc(s_most, 1)
                dve.wait_ge(s_most, 1)
                v.tensor_copy(most_i[:], most[:]).then_inc(s_most, 1)

            def pick_for(dst, E, e, s):
                for t in range(NT):
                    last = v.tensor_scalar(dst[:, t, :], cst[:, C_IOTA:C_IOTA + SLOTS],
                                           place[:, t, bass.ds(e, 1)], None, ALU.is_equal)
                last.then_inc(s, 1)

            def gathered(E):
                dve.wait_ge(s_xg_h, E + 1)
                v.tensor_tensor(xT_l[:, 0:D].rearrange("p (b n) -> p b n", b=2), bank[:, 5:7, :],
                                xT_h[:, 0:D].rearrange("p (b n) -> p b n", b=2).bitcast(F32),
                                ALU.subtract).then_inc(s_xg, 1)

            def combine(E, e):
                dve.wait_ge(s_scatter, E + 1)
                for b in range(4):
                    t, half = b // 2, b % 2
                    part = xres[:, t, half * CHUNK:(half + 1) * CHUNK]
                    last = v.scalar_tensor_tensor(out=part, in0=bank[:, (5, 6, 7, 4)[b], :],
                                                  scalar=egate[:, t, bass.ds(e, 1)], in1=part,
                                                  op0=ALU.mult, op1=ALU.add)
                last.then_inc(s_combined, 1)

            def chunk_hidden(C, n):
                dve.wait_ge(s_esilu, C + 1)
                dve.wait_ge(s_pe, n + 4)
                v.tensor_tensor(hid[:], bank[:, 3, :], silu_g[:], ALU.mult).then_inc(s_ehid, 1)

            def chunk_hT(C):
                dve.wait_ge(s_ehT_h, C + 1)
                v.tensor_tensor(hT_l[:], bank[:, 4, :], hT_h[:].bitcast(F32), ALU.subtract).then_inc(s_ehT, 1)

            def expert(pas, e, first, last):
                E = EXPERTS * pas + e
                C = CHUNKS_E * E
                n = MOE[pas] + EXP_UNITS * e
                for m in range(4):
                    split(n + m + 3, (5 + m + 3) % RAW, m % 3)
                chunk_hidden(C, n)
                if not first:
                    combine(E - 1, e - 1)
                if not (isinstance(E, int) and E == 0):
                    dve.wait_ge(s_pickturn, E)
                pick_for(pick_s, E, e, s_pick_s)
                chunk_hT(C)
                if not last:
                    dve.wait_ge(s_gather, E + 1)
                    pick_for(pick, E + 1, e + 1, s_pick)

                def chunk(c, n1, skip):
                    for m in range(6):
                        if not (skip and m == 5):
                            split(n1 + m + 3, (5 + 4 + m + 3) % RAW, (4 + m) % 3)
                        if m == 3:
                            chunk_hidden(C + c, n1)
                    chunk_hT(C + c)
                chunk(1, n + 4, False)
                with dve.Fori(2, CHUNKS_E - 1 if last else CHUNKS_E) as c:
                    chunk(c, n + 4 + 6 * (c - 1), False)
                if last:
                    chunk(CHUNKS_E - 1, n + EXP_UNITS - 8, True)
                else:
                    gathered(E + 1)
                    for m in range(EXP_UNITS - 2, EXP_UNITS):
                        split(n + m + 3, (5 + m + 3) % RAW, m % 3)
                dve.wait_ge(s_eo_h, E + 1)
                v.tensor_tensor(eo_l.rearrange("p (b n) -> p b n", b=2), bank[:, 0:2, :],
                                eo_h.rearrange("p (b n) -> p b n", b=2).bitcast(F32),
                                ALU.subtract).then_inc(s_eo, 1)

            def experts(pas):
                if pas:
                    dve.wait_ge(s_gather, EXPERTS * pas)
                pick_for(pick, EXPERTS * pas, 0, s_pick)
                gathered(EXPERTS * pas)
                expert(pas, 0, True, False)
                with dve.Fori(1, EXPERTS - 1) as e:
                    expert(pas, e, False, False)
                expert(pas, EXPERTS - 1, False, True)
                combine(EXPERTS * pas + EXPERTS - 1, EXPERTS - 1)

            dve.wait_ge(s_small, 5 * 16)
            v.memset(cu[:], 0.0)
            step(v.tensor_tensor(lamp, lamv[:, 0::2, :, :], lamv[:, 1::2, :, :], ALU.mult))
            step(v.tensor_reduce(lams[:], lamp, AX_X, ALU.add))
            for l in range(LAYERS):
                v.tensor_scalar(sublng[:, l:l + 1], colp[:, LAYERS * KD * TAPS + l:LAYERS * KD * TAPS + l + 1],
                                1.0 - lambda_init(l), None, ALU.mult)
            dve.wait_ge(s_setup_a, 1)
            step(v.tensor_tensor(lamd[:], lame[:, 1, :], lame[:, 0, :], ALU.subtract))
            for l in range(LAYERS):
                last = v.tensor_scalar(neglam[:, l:l + 1], lamd[:, l:l + 1], -lambda_init(l), None, ALU.add)
            step(last)
            norm(0)
            for n in range(4):
                split_unit(n)
            mixer(0)
            for n in range(3):
                split_unit(FFN0 + n)
            residual(OUT0 + OUT_UNITS - 1)
            norm(1)
            ffn()
            residual(FFN0 + FFN_UNITS - 1)
            norm(2)
            mixer(1)
            for n in range(3):
                split_unit(MOE1 + n)
            residual(OUT1 + OUT_UNITS - 1)
            route()
            norm(3)
            top_two()
            experts(0)
            with dve.If(dve.value_load(most_i[0:1, 0:1], min_val=0, max_val=T) > SLOTS):
                for n in range(3):
                    split_unit(MOE2 + n)
                v.tensor_scalar(place[:], place[:], -float(SLOTS), None, ALU.add).then_inc(s_most, 1)
                dve.wait_ge(s_most, 3)
                experts(1)
            v.memset(mark[:], 0.0).then_inc(s_xres, 1)
            norm(4)

        @block.gpsimd
        def _(pool):
            def inv_root(src, mean, dst, per, s_mean, s_out, value):
                nc.gpsimd.tensor_tensor(mean[:], src[:], cst[:, per:per + NT], ALU.mult).then_inc(s_mean, 1)
                pool.wait_ge(s_mean, 2 * value - 1)
                nc.gpsimd.tensor_tensor(mean[:], mean[:], cst[:, C_EPS:C_EPS + NT], ALU.add).then_inc(s_mean, 1)
                pool.wait_ge(s_mean, 2 * value)
                nc.gpsimd.tensor_tensor(dst[:], mean[:], cst[:, C_NH:C_NH + NT], ALU.pow).then_inc(s_out, 1)

            def norm(q):
                pool.wait_ge(s_ss, q + 1)
                inv_root(ss, ms, rstd, C_PER_D, s_ms, s_rstd, q + 1)

            norm(0)
            for l in range(LAYERS):
                with pool.Fori(HEADS * l + 1, HEADS * l + HEADS + 1) as J:
                    pool.wait_ge(s_osq, J)
                    inv_root(osq, oms, orstd, C_PER_VD, s_oms, s_orstd, J)
                norm(2 * l + 1)
                if l == 0:
                    norm(2)
            norm(4)

        @block.tensor
        def _(pe):
            def mm(o, lhsT, rhs, start, stop):
                return nc.tensor.matmul(o, lhsT, rhs, start=start, stop=stop)

            def mm3(o, ah, al, bh, bl, start, stop):
                mm(o, ah, bh, start, False)
                mm(o, ah, bl, False, False)
                return mm(o, al, bh, False, stop)

            def norm(q):
                for t in range(NT):
                    pe.wait_ge(s_normed, NT * q + t + 1)
                    for half in range(2):
                        for k in range(4):
                            kk = 4 * half + k
                            last = nc.tensor.transpose(bank[:, 4 + 2 * t + half, k * P:(k + 1) * P],
                                                       normed_x[:, t, kk * P:(kk + 1) * P], ident)
                        last.then_inc(s_turned, 1)

            def attention_a(J):
                pe.wait_ge(s_pdiff, J)
                for i in range(3):
                    last = nc.tensor.transpose(bank[:, 6, i * P:(i + 1) * P], pdiff[:, i * P:(i + 1) * P], ident)
                last.then_inc(s_pturn, 1)

            def attention_b(J, B7_used):
                pe.wait_ge(s_pT, J)
                pe.wait_ge(s_vb, J)
                if B7_used:
                    pe.wait_ge(s_mix2, J - 1)
                mm(bank[:, 7, 0:P], pT[:, 0:P], vb[:, 0:P], True, True)
                mm(bank[:, 7, P:2 * P], pT[:, P:2 * P], vb[:, 0:P], True, False)
                mm(bank[:, 7, P:2 * P], pT[:, 2 * P:3 * P], vb[:, P:2 * P], False, True).then_inc(s_pv, 1)

            def attention_c(J):
                pe.wait_ge(s_onorm, J)
                for t in range(NT):
                    last = nc.tensor.transpose(bank[:, 7, T + t * P:T + (t + 1) * P], onorm[:, t * P:(t + 1) * P], ident)
                last.then_inc(s_oturn, 1)

            def qk_scores(J):
                pe.wait_ge(s_roped, J + 1)
                if not (isinstance(J, int) and J == 0):
                    pe.wait_ge(s_nmax, J)
                for m in range(2):
                    rows = slice(HD * m, HD * (m + 1))
                    mm(bank[:, 4 + m, 0:P], qkT[rows, 0:P], qkT[rows, T:T + P], True, True)
                    last = mm(bank[:, 4 + m, P:3 * P], qkT[rows, P:2 * P], qkT[rows, T:2 * T], True, True)
                last.then_inc(s_scores, 1)

            def projection(b, off, u, s):
                wh, wl = block_of(hi, u, s=2, k=KD), block_of(lo, u, s=2, k=KD)
                for k in range(KD):
                    last = mm3(bank[:, b, off:off + T], wh[:, s, k, :], wl[:, s, k, :], xTh[:, k, :], xTl[:, k, :],
                               k == 0, k == KD - 1)
                return last

            def head(l, j):
                J = HEADS * l + j
                first = isinstance(j, int) and j == 0
                never = first and l == 0
                n = MIX[l] + 4 * j
                pe.wait_ge(s_lo, n + 1)
                if not never:
                    pe.wait_ge(s_roped, J)
                projection(0, 0, 0, 0)
                projection(0, T, 0, 1).then_inc(s_pe, 1)
                if not first:
                    attention_a(J)
                pe.wait_ge(s_lo, n + 2)
                if not never:
                    pe.wait_ge(s_vb, J)
                wh, wl = block_of(hi, 1, s=2, k=KD), block_of(lo, 1, s=2, k=KD)
                for t in range(NT):
                    tok = slice(t * P, (t + 1) * P)
                    for k in range(KD):
                        mm3(bank[:, 1, tok], xTh[:, k, tok], xTl[:, k, tok], wh[:, 0, k, :], wl[:, 0, k, :],
                            k == 0, k == KD - 1)
                projection(1, T, 1, 1).then_inc(s_pe, 1)
                if not first:
                    attention_b(J, True)
                qk_scores(J)
                pe.wait_ge(s_lo, n + 3)
                if not never:
                    pe.wait_ge(s_conv, J)
                projection(2, 0, 2, 0)
                projection(2, T, 2, 1).then_inc(s_pe, 1)
                if not first:
                    attention_c(J)
                pe.wait_ge(s_lo, n + 4)
                if not never:
                    pe.wait_ge(s_gates, J)
                projection(3, 0, 3, 0)
                projection(3, T, 3, 1).then_inc(s_pe, 1)

            def mixer(l):
                pe.wait_ge(s_xt, 4 * 2 * l + 4)
                head(l, 0)
                if l == 0:
                    head_one(l)
                with pe.Fori(2 if l == 0 else 1, HEADS) as j:
                    head(l, j)
                J = HEADS * (l + 1)
                attention_a(J)
                attention_b(J, True)
                attention_c(J)
                pe.wait_ge(s_mT, J)
                pe.wait_ge(s_gates, J)
                for u in range(OUT_UNITS):
                    pe.wait_ge(s_lo, OUT[l] + u + 1)
                    wh, wl = block_of(hi, u, k=2), block_of(lo, u, k=2)
                    for kk in range(2):
                        k = 2 * u + kk
                        for b in range(4):
                            tok, ch = slice((b // 2) * P, (b // 2 + 1) * P), slice((b % 2) * CHUNK, (b % 2 + 1) * CHUNK)
                            last = mm3(bank[:, b, :], mTh[:, k, tok], mTl[:, k, tok], wh[:, kk, ch], wl[:, kk, ch],
                                       k == 0, k == KD - 1)
                    last.then_inc(s_pe, 1)

            def head_one(l):
                head(l, 1)

            def ffn_cols(b, part):
                wh, wl = block_of(hi, part, k=KD), block_of(lo, part, k=KD)
                for f in range(2):
                    for k in range(KD):
                        cols_f = slice(f * P, (f + 1) * P)
                        last = mm3(bank[:, b, f * T:(f + 1) * T], wh[:, k, cols_f], wl[:, k, cols_f],
                                   xTh[:, k, :], xTl[:, k, :], k == 0, k == KD - 1)
                last.then_inc(s_pe, 1)

            def ffn_down(i, n, part, first, final):
                pe.wait_ge(s_lo, n + 1)
                pe.wait_ge(s_fhT, i + 1)
                wh, wl = block_of(hi, part, r=2), block_of(lo, part, r=2)
                for f in range(2):
                    for b in range(4):
                        tok = slice(f * T + (b // 2) * P, f * T + (b // 2 + 1) * P)
                        ch = slice((b % 2) * CHUNK, (b % 2 + 1) * CHUNK)
                        last = mm3(bank[:, b, :], hT_h[:, tok], hT_l[:, tok], wh[:, f, ch], wl[:, f, ch],
                                   first and f == 0, final and f == 1)
                last.then_inc(s_pe, 1)

            def ffn_pair(i, first_down=False):
                n = FFN0 + 3 * i - 1
                pe.wait_ge(s_lo, n + 1)
                pe.wait_ge(s_fsilu, i)
                ffn_cols(4, 2)
                pe.wait_ge(s_lo, n + 2)
                pe.wait_ge(s_fhid, i)
                ffn_cols(5, 0)
                ffn_down(i - 1, n + 2, 1, first_down, False)

            def ffn():
                pe.wait_ge(s_xt, 8)
                pe.wait_ge(s_lo, FFN0 + 1)
                ffn_cols(4, 0)
                pe.wait_ge(s_lo, FFN0 + 2)
                ffn_cols(5, 1)
                ffn_pair(1, True)
                with pe.Fori(2, PAIRS) as i:
                    ffn_pair(i)
                ffn_down(PAIRS - 1, FFN0 + FFN_UNITS - 1, (FFN_UNITS - 1) % 3, False, True)

            def route():
                pe.wait_ge(s_xt, 16)
                pe.wait_ge(s_rw, 1)
                rh = rw_h[:].rearrange("p (k e) -> p k e", k=KD)
                rl = rw_l[:].rearrange("p (k e) -> p k e", k=KD)
                for t in range(NT):
                    tok = slice(t * P, (t + 1) * P)
                    for k in range(KD):
                        last = mm3(bank[:, 0, t * EXPERTS:(t + 1) * EXPERTS], xTh[:, k, tok], xTl[:, k, tok],
                                   rh[:, k, :], rl[:, k, :], k == 0, k == KD - 1)
                last.then_inc(s_logit, 1)
                pe.wait_ge(s_chosen, 1)
                upper, ones = cst[:, C_UPPER:C_UPPER + P], cst[:, C_ONES:C_ONES + P]
                E = EXPERTS
                mm(bank[:, 1, 0:E], upper, chosen[:, 0, :], True, True)
                mm(bank[:, 1, E:2 * E], ones, chosen[:, 0, :], True, False)
                mm(bank[:, 1, E:2 * E], upper, chosen[:, 1, :], False, True)
                mm(bank[:, 1, 2 * E:3 * E], ones, chosen[:, 0, :], True, False)
                mm(bank[:, 1, 2 * E:3 * E], ones, chosen[:, 1, :], False, True).then_inc(s_count, 1)

            def gather(E):
                pe.wait_ge(s_pick, E + 1)
                if not (isinstance(E, int) and E <= 1):
                    pe.wait_ge(s_combined, E - 1)
                for k in range(KD):
                    o = bank[:, 5 + k // 4, (k % 4) * SLOTS:(k % 4 + 1) * SLOTS]
                    d = slice(k * P, (k + 1) * P)
                    for t in range(NT):
                        mm(o, nxh[:, t, d], pick[:, t, :], t == 0, False)
                        last = mm(o, nxl[:, t, d], pick[:, t, :], False, t == NT - 1)
                last.then_inc(s_gather, 1)

            def scatter(E):
                pe.wait_ge(s_eo, E + 1)
                pe.wait_ge(s_pickT, E + 1)
                for b in range(4):
                    o = bank[:, (5, 6, 7, 4)[b], :]
                    tok, ch = slice((b // 2) * P, (b // 2 + 1) * P), slice((b % 2) * CHUNK, (b % 2 + 1) * CHUNK)
                    mm(o, pickT[:, tok], eo_h[:, ch], True, False)
                    last = mm(o, pickT[:, tok], eo_l[:, ch], False, True)
                last.then_inc(s_scatter, 1)

            def expert_cols(b, n, at):
                for half in range(2):
                    part = (at + half) % 3
                    pe.wait_ge(s_lo, n + half + 1)
                    wh, wl = block_of(hi, part, k=4), block_of(lo, part, k=4)
                    for kk in range(4):
                        k = 4 * half + kk
                        last = mm3(bank[:, b, :], xgh[:, k, :], xgl[:, k, :], wh[:, kk, :], wl[:, kk, :],
                                   k == 0, k == KD - 1)
                    last.then_inc(s_pe, 1)

            def turn_hidden(C):
                pe.wait_ge(s_ehid, C + 1)
                for f in range(4):
                    last = nc.tensor.transpose(bank[:, 4, f * P:(f + 1) * P], hid[:, f * P:(f + 1) * P], ident)
                last.then_inc(s_ehturn, 1)

            def expert_down(C, n, at, first, final):
                pe.wait_ge(s_ehT, C + 1)
                for half in range(2):
                    part = (at + half) % 3
                    pe.wait_ge(s_lo, n + half + 1)
                    wh, wl = block_of(hi, part, r=2), block_of(lo, part, r=2)
                    for r in range(2):
                        f = 2 * half + r
                        rows = slice(f * SLOTS, (f + 1) * SLOTS)
                        for b in range(2):
                            ch = slice(b * CHUNK, (b + 1) * CHUNK)
                            last = mm3(bank[:, b, :], hT_h[:, rows], hT_l[:, rows], wh[:, r, ch], wl[:, r, ch],
                                       first and f == 0, final and f == 3)
                    last.then_inc(s_pe, 1)

            def expert_chunk(C, n, at, first):
                if not (isinstance(C, int) and C == 0):
                    pe.wait_ge(s_esilu, C)
                expert_cols(2, n, at)
                if not (isinstance(C, int) and C == 0):
                    pe.wait_ge(s_ehid, C)
                expert_cols(3, n + 2, at + 2)

            def expert(pas, e, first, last):
                E = EXPERTS * pas + e
                C = CHUNKS_E * E
                n = MOE[pas] + EXP_UNITS * e
                pe.wait_ge(s_xg, E + 1)
                expert_chunk(C, n, 0, True)
                if not first:
                    scatter(E - 1)
                    pe.wait_ge(s_combined, E)
                turn_hidden(C)
                expert_chunk(C + 1, n + 4, 4, False)
                if not (isinstance(E, int) and E == 0):
                    pe.wait_ge(s_eo, E)
                expert_down(C, n + 8, 8, True, False)
                turn_hidden(C + 1)
                with pe.Fori(2, CHUNKS_E) as c:
                    n1 = n + 4 + 6 * (c - 1)
                    expert_chunk(C + c, n1, 4, False)
                    expert_down(C + c - 1, n1 + 4, 8, False, False)
                    turn_hidden(C + c)
                pe.wait_ge(s_pick_s, E + 1)
                for t in range(NT):
                    turned = nc.tensor.transpose(bank[:, 7, t * P:(t + 1) * P], pick_s[:, t, :], ident)
                turned.then_inc(s_pickturn, 1)
                if not last:
                    gather(E + 1)
                expert_down(C + CHUNKS_E - 1, n + EXP_UNITS - 2, EXP_UNITS - 2, False, True)

            def experts(pas):
                gather(EXPERTS * pas)
                expert(pas, 0, True, False)
                with pe.Fori(1, EXPERTS - 1) as e:
                    expert(pas, e, False, False)
                expert(pas, EXPERTS - 1, False, True)
                scatter(EXPERTS * pas + EXPERTS - 1)

            norm(0)
            mixer(0)
            norm(1)
            ffn()
            norm(2)
            mixer(1)
            norm(3)
            route()
            pe.wait_ge(s_nx, NT)
            experts(0)
            pe.wait_ge(s_most, 2)
            with pe.If(pe.value_load(most_i[0:1, 0:1], min_val=0, max_val=T) > SLOTS):
                pe.wait_ge(s_combined, EXPERTS)
                experts(1)


def constants():
    import numpy as np

    f = np.float32
    c = np.zeros((P, C_ALL), f)
    c[:, C_ID:C_ID + P] = np.eye(P, dtype=f)
    inv = (f(1.0) / (f(THETA) ** (np.arange(0, HD, 2, dtype=f) / f(HD)))).astype(f)
    ang = np.arange(T, dtype=f)[None, :] * inv[:, None]
    cos, sin = np.cos(ang).astype(f), np.sin(ang).astype(f)
    for q in range(4):
        rows = slice(32 * q, 32 * q + 32)
        c[rows, C_COS:C_COS + T] = cos
        c[rows, C_SIN:C_SIN + T] = sin if q % 2 == 0 else -sin
    row, col = np.arange(P)[:, None], np.arange(P)[None, :]
    future = np.where(col > row, f(-3e38), f(0))
    c[:, C_MASK:C_MASK + P] = future
    c[:, C_MASK + 2 * P:C_MASK + 3 * P] = future
    c[:, C_UPPER:C_UPPER + P] = (row < col)
    c[:, C_ONES:C_ONES + P] = 1
    c[:, C_IOTA:C_IOTA + SLOTS] = np.arange(SLOTS)
    e = np.arange(EXPERTS)
    c[:, C_TRI:C_TRI + EXPERTS ** 2] = (e[None, :] < e[:, None]).reshape(-1)
    c[:, C_NH:C_NH + NT] = -0.5
    c[:, C_EPS:C_EPS + NT] = EPS
    c[:, C_PER_D:C_PER_D + NT] = 1 / D
    c[:, C_PER_VD:C_PER_VD + NT] = 1 / VD
    return c


def build(nc, arrays):
    ins = {n: nc.dram_tensor(n, a.shape, F32, kind="ExternalInput").ap() for n, a in arrays.items()}
    out = nc.dram_tensor("out", (T, D), F32, kind="ExternalOutput").ap()
    hybrid_trunk(nc, *ins.values(), out)


def layout(i):
    import numpy as np

    c = np.ascontiguousarray
    a = {n: np.asarray(x) for n, x in i.items()}
    taps = a["conv_w"].reshape(LAYERS, TAPS, KD, P).transpose(3, 0, 2, 1).reshape(P, -1)
    return {
        "x": c(a["x"].reshape(T, D)),
        "w_in": c(a["w_in"]),
        "w_out": c(a["w_out"]),
        "gains": c(np.stack([a["norm_mix"][0], a["norm_ffn"][0], a["norm_mix"][1], a["norm_ffn"][1], a["norm_final"]])),
        "lam_rows": c(np.stack([a["lam_q1"], a["lam_k1"], a["lam_q2"], a["lam_k2"]]).reshape(1, -1)),
        "cols": c(np.concatenate([taps, a["subln_g"].T], axis=1)),
        "router": c(a["router_w"][0].reshape(KD, P, EXPERTS).transpose(1, 0, 2).reshape(P, -1)),
        "w_gate": c(a["ffn_w_gate"]),
        "w_up": c(a["ffn_w_up"]),
        "w_down": c(a["ffn_w_down"]),
        "e_gate": c(a["exp_w_gate"]),
        "e_up": c(a["exp_w_up"]),
        "e_down": c(a["exp_w_down"]),
        "consts": constants(),
    }


def kernel(**inputs):
    import concourse.bacc as bacc
    from concourse.bass_utils import run_bass_kernel_spmd

    nc = bacc.Bacc("TRN2", target_bir_lowering=False, num_devices=1)
    arrays = layout(inputs)
    build(nc, arrays)
    r = run_bass_kernel_spmd(nc, [arrays], core_ids=[0])
    return r.results[0]["out"].reshape(1, T, D)
```

```python
import math
from contextlib import ExitStack

import concourse.bass as bass
from concourse import mybir

F32 = mybir.dt.float32
F32R = mybir.dt.float32r
BF16 = mybir.dt.bfloat16
I32 = mybir.dt.int32
ALU = mybir.AluOpType
ACT = mybir.ActivationFunctionType
AX_X = mybir.AxisListType.X

P = 128
D = 1024
T = 256
LAYERS = 2
HEADS = 8
HD = 64
VD = 2 * HD
F_DENSE = 2816
F_EXPERT = 3584
EXPERTS = 8
TAPS = 3
EPS = 1e-5
THETA = 10000.0
KD = D // P
NT = T // P
SLOTS = P
CHUNK = 512
NCH = D // CHUNK
CHUNKS_E = F_EXPERT // CHUNK
PAIRS = F_DENSE // (2 * P)
RW_COLS = (KD - 1) * EXPERTS + P

UNIT = 2048
RAW = 6
SPLIT = 4
MIX_UNITS = 4 * HEADS
OUT_UNITS = 4
FFN_UNITS = 3 * PAIRS
EXP_UNITS = 6 * CHUNKS_E
MIX0 = 0
OUT0 = MIX0 + MIX_UNITS
FFN0 = OUT0 + OUT_UNITS
MIX1 = FFN0 + FFN_UNITS
OUT1 = MIX1 + MIX_UNITS
MOE1 = OUT1 + OUT_UNITS
MOE2 = MOE1 + EXPERTS * EXP_UNITS
MIX = (MIX0, MIX1)
OUT = (OUT0, OUT1)
MOE = (MOE1, MOE2)
RAW_FIRST = {MIX0: 0, OUT0: 0, FFN0: 4, MIX1: 1, OUT1: 1, MOE1: 5, MOE2: 5}

C_ID = 0
C_NH = C_ID + P
C_EPS = C_NH + NT
C_PER_D = C_EPS + NT
C_PER_VD = C_PER_D + NT
C_FIRST = C_PER_VD + NT
C_COS = C_FIRST
C_SIN = C_COS + T
C_MASK = C_SIN + T
C_UPPER = C_MASK + 3 * P
C_ONES = C_UPPER + P
C_IOTA = C_ONES + P
C_TRI = C_IOTA + SLOTS
C_ALL = C_TRI + EXPERTS * EXPERTS


def lambda_init(layer):
    return 0.8 - 0.6 * math.exp(-0.3 * layer)


def unit_info(n):
    counts = [0] * RAW
    for m in range(n + 1):
        base = max(b for b in RAW_FIRST if b <= m)
        i = m - base
        four = base in (MIX0, MIX1, OUT0, OUT1)
        slot = RAW_FIRST[base] + i % 4 if four else (RAW_FIRST[base] + i) % RAW
        counts[slot] += 32 if base in MIX else 16
    return slot, (i % 4 if four else i % 3), counts[slot]


def raw_users():
    last, before = [-1] * RAW, []
    for m in range(MOE1 + RAW):
        s = unit_info(m)[0]
        before.append(last[s])
        last[s] = m
    return before


BEFORE = raw_users()


def hybrid_trunk(nc, x, w_in, w_out, gains, lam_rows, cols, router, w_gate, w_up, w_down,
                 e_gate, e_up, e_down, consts, out):
    with ExitStack() as ctx:
        def sb(name, shape, dt=F32):
            return ctx.enter_context(nc.sbuf_tensor(name, shape, dt))

        def sem(name):
            return ctx.enter_context(nc.semaphore(name))

        raw = sb("raw", [P, RAW, UNIT])
        hi = sb("hi", [P, SPLIT, UNIT], F32R)
        lo = sb("lo", [P, SPLIT, UNIT], F32R)
        xres = sb("xres", [P, NT, D])
        normed_x = sb("normed_x", [P, NT, D])
        xT_h = sb("xT_h", [P, KD * T], F32R)
        xT_l = sb("xT_l", [P, KD * T], F32R)
        mT_h = sb("mT_h", [P, KD * T], F32R)
        mT_l = sb("mT_l", [P, KD * T], F32R)
        gain = sb("gain", [P, D])
        cst = sb("cst", [P, C_ALL])
        colp = sb("colp", [P, LAYERS * KD * TAPS + LAYERS])
        sublng = sb("sublng", [P, LAYERS])
        lams = sb("lams", [P, 2, LAYERS])
        lame = sb("lame", [P, 2, LAYERS])
        lamd = sb("lamd", [P, LAYERS])
        neglam = sb("neglam", [P, LAYERS])
        ss = sb("ss", [P, NT])
        ms = sb("ms", [P, NT])
        rstd = sb("rstd", [P, NT])
        rope_s = sb("rope_s", [P, 2 * T])
        rope_c = sb("rope_c", [P, 2 * T])
        qkT = sb("qkT", [P, 2 * T])
        vb = sb("vb", [P, 2 * T])
        v_tok = sb("v_tok", [P, T])
        c_sb = sb("c_sb", [P, T])
        cu = sb("cu", [P, T + TAPS - 1])
        conv = sb("conv", [P, T])
        yconv = sb("yconv", [P, T])
        gates_t = sb("gates_t", [P, 2 * T])
        cgated = sb("cgated", [P, T])
        agated = sb("agated", [P, T])
        mix2 = sb("mix2", [P, T])
        scores = sb("scores", [P, 2, 3 * P])
        smax = sb("smax", [P, 4])
        nmax = sb("nmax", [P, 4])
        ssum = sb("ssum", [P, 4])
        srec = sb("srec", [P, 4])
        srec1 = sb("srec1", [P, 2])
        pm1 = sb("pm1", [P, 3 * P])
        pdiff = sb("pdiff", [P, 3 * P])
        pT = sb("pT", [P, 3 * P])
        osq = sb("osq", [P, NT])
        oms = sb("oms", [P, NT])
        orstd = sb("orstd", [P, NT])
        onorm = sb("onorm", [P, T])
        hT_h = sb("hT_h", [P, CHUNK], F32R)
        hT_l = sb("hT_l", [P, CHUNK], F32R)
        rw = sb("rw", [P, RW_COLS])
        rw_h = sb("rw_h", [P, RW_COLS], F32R)
        rw_l = sb("rw_l", [P, RW_COLS], F32R)
        logitT = sb("logitT", [EXPERTS, T])
        logit = sb("logit", [P, NT, EXPERTS])
        rank = sb("rank", [P, NT, EXPERTS])
        top1 = sb("top1", [P, NT, EXPERTS])
        top2 = sb("top2", [P, NT, EXPERTS])
        v1 = sb("v1", [P, NT])
        v2 = sb("v2", [P, NT])
        v2e = sb("v2e", [P, NT])
        den = sb("den", [P, NT])
        w1 = sb("w1", [P, NT])
        w2 = sb("w2", [P, NT])
        chosen = sb("chosen", [P, NT, EXPERTS])
        egate = sb("egate", [P, NT, EXPERTS])
        place = sb("place", [P, NT, EXPERTS])
        most = sb("most", [P, 1])
        most_i = sb("most_i", [P, 1], I32)
        pick = sb("pick", [P, NT, SLOTS], F32R)
        pickT = sb("pickT", [P, T], F32R)
        mark = sb("mark", [P, 1])
        warm = sb("warm", [P, NT])

        bank = ctx.enter_context(nc.psum_tensor("bank", [P, 8, CHUNK], F32))

        landed = [sem(f"landed{i}") for i in range(RAW)]
        s_x = [sem(f"s_x{t}") for t in range(NT)]
        s_const = sem("s_const")
        s_small = sem("s_small")
        s_out = sem("s_out")
        s_gain = sem("s_gain")
        s_hi = sem("s_hi")
        s_lo = sem("s_lo")
        s_pe = sem("s_pe")
        s_setup = sem("s_setup")
        s_setup_a = sem("s_setup_a")
        s_setup_p = sem("s_setup_p")
        s_ss = sem("s_ss")
        s_ms = sem("s_ms")
        s_rstd = sem("s_rstd")
        s_normed = sem("s_normed")
        s_turned = sem("s_turned")
        s_xt_h = sem("s_xt_h")
        s_xt = sem("s_xt")
        s_xres = sem("s_xres")
        s_rope1 = sem("s_rope1")
        s_roped = sem("s_roped")
        s_scores = sem("s_scores")
        s_masked = sem("s_masked")
        s_maxed = sem("s_maxed")
        s_nmax = sem("s_nmax")
        s_exp = sem("s_exp")
        s_srec = sem("s_srec")
        s_srec1 = sem("s_srec1")
        s_pm1 = sem("s_pm1")
        s_pdiff = sem("s_pdiff")
        s_pturn = sem("s_pturn")
        s_pT = sem("s_pT")
        s_vb = sem("s_vb")
        s_vturn = sem("s_vturn")
        s_v = sem("s_v")
        s_pv = sem("s_pv")
        s_osq = sem("s_osq")
        s_oms = sem("s_oms")
        s_orstd = sem("s_orstd")
        s_onorm = sem("s_onorm")
        s_oturn = sem("s_oturn")
        s_c = sem("s_c")
        s_cu = sem("s_cu")
        s_tap = sem("s_tap")
        s_conv = sem("s_conv")
        s_gates = sem("s_gates")
        s_agated = sem("s_agated")
        s_mix2 = sem("s_mix2")
        s_cgated = sem("s_cgated")
        s_mT_h = sem("s_mT_h")
        s_mT = sem("s_mT")
        s_fsilu = sem("s_fsilu")
        s_fhid = sem("s_fhid")
        s_fhT_h = sem("s_fhT_h")
        s_fhT = sem("s_fhT")
        s_rw_h = sem("s_rw_h")
        s_rw = sem("s_rw")
        s_nx_h = sem("s_nx_h")
        s_nx = sem("s_nx")
        s_logit = sem("s_logit")
        s_route = sem("s_route")
        s_v2e = sem("s_v2e")
        s_chosen = sem("s_chosen")
        s_count = sem("s_count")
        s_most = sem("s_most")
        s_esilu = sem("s_esilu")
        s_ehid = sem("s_ehid")
        s_ehturn = sem("s_ehturn")
        s_ehT_h = sem("s_ehT_h")
        s_ehT = sem("s_ehT")
        s_pick = sem("s_pick")
        s_pick_s = sem("s_pick_s")
        s_gather = sem("s_gather")
        s_xg_h = sem("s_xg_h")
        s_xg = sem("s_xg")
        s_pickturn = sem("s_pickturn")
        s_pickT = sem("s_pickT")
        s_half = sem("s_half")
        s_eo_h = sem("s_eo_h")
        s_eo = sem("s_eo")
        s_scatter = sem("s_scatter")
        s_combined = sem("s_combined")
        s_stored = sem("s_stored")

        ident = cst[:, C_ID:C_ID + P]
        xTh = xT_h[:].rearrange("p (k t) -> p k t", k=KD)
        xTl = xT_l[:].rearrange("p (k t) -> p k t", k=KD)
        mTh = mT_h[:].rearrange("p (k t) -> p k t", k=KD)
        mTl = mT_l[:].rearrange("p (k t) -> p k t", k=KD)
        nxh = mT_h[:].rearrange("p (t d) -> p t d", t=NT)
        nxl = mT_l[:].rearrange("p (t d) -> p t d", t=NT)
        xgh = xT_h[:, 0:KD * SLOTS].rearrange("p (k s) -> p k s", k=KD)
        xgl = xT_l[:, 0:KD * SLOTS].rearrange("p (k s) -> p k s", k=KD)

        lamv = scores[:].rearrange("p m n -> p (m n)")[:, 0:4 * LAYERS * HD].rearrange(
            "p (a l d) -> p a l d", a=4, l=LAYERS)
        lamp = pdiff[:, 0:2 * LAYERS * HD].rearrange("p (a l d) -> p a l d", a=2, l=LAYERS)
        silu_g, hid = rope_s, rope_c
        above, ties = (b[:, 0:NT * EXPERTS * EXPERTS].rearrange("p (t e j) -> p t e j", t=NT, e=EXPERTS)
                       for b in (conv, yconv))
        pick_s = gates_t[:, 0:NT * SLOTS].rearrange("p (t s) -> p t s", t=NT)
        eo_h = xT_h[:, KD * SLOTS:KD * SLOTS + D]
        eo_l = xT_l[:, KD * SLOTS:KD * SLOTS + D]

        def block_of(buf, slot, **sizes):
            pattern = "p (" + " ".join(sizes) + " n) -> p " + " ".join(sizes) + " n"
            return buf[:, slot, :].rearrange(pattern, **sizes)

        block = ctx.enter_context(nc.Block())

        @block.sync
        def _(sp):
            w_in_v = [w_in[l].rearrange("(k p) n -> p k n", p=P) for l in range(LAYERS)]
            w_out_v = [w_out[l].rearrange("(k p) n -> p k n", p=P) for l in range(LAYERS)]
            gate_v = w_gate.rearrange("a (k p) f -> p (a k) f", p=P)
            up_v = w_up.rearrange("a (k p) f -> p (a k) f", p=P)
            down_v = w_down.rearrange("a (r p) n -> p (a r) n", p=P)
            egate_v = e_gate.rearrange("a e (k p) f -> p (a e k) f", p=P)
            eup_v = e_up.rearrange("a e (k p) f -> p (a e k) f", p=P)
            edown_v = e_down.rearrange("a e (r p) n -> p (a e r) n", p=P)

            def load_gain(q):
                if q:
                    sp.wait_ge(s_normed, NT * q)
                sp.dma_start(gain[:], gains[q:q + 1, :].to_broadcast([P, D])).then_inc(s_gain, 16)

            def load_mixer(l, j, u, slot):
                for s in range(2):
                    part = raw[:, slot, s * (UNIT // 2):(s + 1) * (UNIT // 2)].rearrange("p (k c) -> p k c", k=KD)
                    sp.dma_start(part, w_in_v[l][:, :, bass.ds((2 * u + s) * D + j * P, P)]).then_inc(landed[slot], 16)

            def small_loads():
                sp.dma_start(cst[:, C_FIRST:], consts[:, C_FIRST:]).then_inc(s_small, 16)
                sp.dma_start(colp[:], cols).then_inc(s_small, 16)
                sp.dma_start(rw[:, 0:KD * EXPERTS], router).then_inc(s_small, 16)
                sp.dma_start(lamv.rearrange("p a l d -> p (a l d)"),
                             lam_rows.to_broadcast([P, 4 * LAYERS * HD])).then_inc(s_small, 16)

            def mixer_loads(l):
                for u in range(4):
                    before = BEFORE[MIX[l] + u]
                    if before >= 0:
                        sp.wait_ge(s_lo, before + 1)
                    load_mixer(l, 0, u, RAW_FIRST[MIX[l]] + u)
                    if l == 0 and u == 1:
                        small_loads()
                with sp.Fori(1, HEADS) as j:
                    for u in range(4):
                        sp.wait_ge(s_lo, MIX[l] + 4 * j + u - 3)
                        load_mixer(l, j, u, RAW_FIRST[MIX[l]] + u)

            def out_loads(l):
                for u in range(OUT_UNITS):
                    slot = unit_info(OUT[l] + u)[0]
                    sp.wait_ge(s_lo, BEFORE[OUT[l] + u] + 1)
                    sp.dma_start(block_of(raw, slot, k=2), w_out_v[l][:, 2 * u:2 * u + 2, :]).then_inc(landed[slot], 16)

            def ffn_load(kind, i, slot):
                if kind == "d":
                    dst, src = block_of(raw, slot, r=2), down_v[:, bass.ds(2 * i, 2), :]
                else:
                    dst, src = block_of(raw, slot, k=KD), (gate_v if kind == "g" else up_v)[:, :, bass.ds(i * 2 * P, 2 * P)]
                sp.dma_start(dst, src).then_inc(landed[slot], 16)

            def ffn_loads():
                first = [("g", 0), ("u", 0), ("g", 1), ("u", 1), ("d", 0), ("g", 2), ("u", 2), ("d", 1)]
                for n, (kind, i) in enumerate(first):
                    before = BEFORE[FFN0 + n]
                    if before >= 0:
                        sp.wait_ge(s_lo, before + 1)
                    ffn_load(kind, i, unit_info(FFN0 + n)[0])
                with sp.Fori(0, (PAIRS - 3) // 2) as r:
                    for m in range(6):
                        n = len(first) + m
                        sp.wait_ge(s_lo, FFN0 + n - RAW + 1 + 6 * r)
                        i = 3 + m // 3
                        ffn_load("gud"[m % 3], 2 * r + (i if m % 3 < 2 else i - 1), unit_info(FFN0 + n)[0])
                n = FFN_UNITS - 1
                sp.wait_ge(s_lo, FFN0 + n - RAW + 1)
                ffn_load("d", PAIRS - 1, unit_info(FFN0 + n)[0])

            def expert_units(n, e, c, kinds):
                for m, kind in enumerate(kinds):
                    half = m % 2
                    slot = (5 + m if kinds == "gguu" else 5 + 4 + m) % RAW
                    sp.wait_ge(s_lo, n + m - RAW + 1)
                    if kind == "d":
                        src = edown_v[:, bass.ds(e * (F_EXPERT // P) + 4 * (c - 1) + 2 * half, 2), :]
                        dst = block_of(raw, slot, r=2)
                    else:
                        v = egate_v if kind == "g" else eup_v
                        src = v[:, bass.ds(e * KD + 4 * half, 4), bass.ds(c * CHUNK, CHUNK)]
                        dst = block_of(raw, slot, k=4)
                    sp.dma_start(dst, src).then_inc(landed[slot], 16)

            def expert_loads(start):
                expert_units(start, 0, 0, "gguu")
                with sp.Fori(1, CHUNKS_E) as c:
                    expert_units(start - 2 + 6 * c, 0, c, "gguudd")
                with sp.Fori(1, EXPERTS) as e:
                    with sp.Fori(0, CHUNKS_E) as c:
                        expert_units(start - 2 + EXP_UNITS * e + 6 * c, e, c, "gguudd")
                n = start - 2 + EXP_UNITS * EXPERTS
                for half in range(2):
                    slot = (5 + 4 + half) % RAW
                    sp.wait_ge(s_lo, n + half - RAW + 1)
                    r0 = EXPERTS * (F_EXPERT // P) - 4 + 2 * half
                    sp.dma_start(block_of(raw, slot, r=2), edown_v[:, r0:r0 + 2, :]).then_inc(landed[slot], 16)

            for t in range(NT):
                sp.dma_start(xres[:, t, :], x[t * P:(t + 1) * P, :]).then_inc(s_x[t], 16)
            sp.dma_start(cst[:, 0:C_FIRST], consts[:, 0:C_FIRST]).then_inc(s_const, 16)
            load_gain(0)
            mixer_loads(0)
            load_gain(1)
            out_loads(0)
            ffn_loads()
            load_gain(2)
            mixer_loads(1)
            load_gain(3)
            out_loads(1)
            expert_loads(MOE1)
            load_gain(4)
            sp.wait_ge(s_most, 2)
            with sp.If(sp.value_load(most_i[0:1, 0:1], min_val=0, max_val=T) > SLOTS):
                expert_loads(MOE2)
            for t in range(NT):
                sp.wait_ge(s_normed, NT * 4 + t + 1)
                sp.dma_start(out[t * P:(t + 1) * P, :], normed_x[:, t, :]).then_inc(s_stored, 16)
            sp.wait_ge(s_stored, 16 * NT)

        @block.scalar
        def _(act):
            def copy(dst, src, s, scale=1.0):
                nc.scalar.activation(dst, src, ACT.Copy, scale=scale).then_inc(s, 1)

            def split(slot, part, count, used):
                act.wait_ge(landed[slot], count)
                if used is not None:
                    act.wait_ge(s_pe, used)
                copy(hi[:, part, :], raw[:, slot, :], s_hi)

            def split_unit(n, used):
                slot, part, count = unit_info(n)
                split(slot, part, count, used)

            def norm(q, between=None):
                for t in range(NT):
                    if q == 0:
                        act.wait_ge(s_x[t], 16)
                    else:
                        act.wait_ge(s_xres, NT * (q - 1) + t + 1)
                    nc.scalar.activation(normed_x[:, t, :], xres[:, t, :], ACT.Square,
                                         accum_out=ss[:, t:t + 1]).then_inc(s_ss, 1)
                if q == 4:
                    return
                for b in range(4):
                    t, half = b // 2, b % 2
                    if b == 2 and between is not None:
                        between()
                    act.wait_ge(s_turned, 4 * q + b + 1)
                    copy(xTh[:, 4 * half:4 * half + 4, t * P:(t + 1) * P],
                         bank[:, 4 + b, :].rearrange("p (k t) -> p k t", k=4), s_xt_h)
                if q == 3:
                    for t in range(NT):
                        copy(nxh[:, t, :], normed_x[:, t, :], s_nx_h)

            def attention_a(J):
                act.wait_ge(s_pturn, J)
                copy(pT[:], bank[:, 6, 0:3 * P], s_pT)

            def attention_b(J):
                act.wait_ge(s_pv, J)
                for t in range(NT):
                    last = nc.scalar.activation(onorm[:, t * P:(t + 1) * P], bank[:, 7, t * P:(t + 1) * P],
                                                ACT.Square, accum_out=osq[:, t:t + 1])
                last.then_inc(s_osq, 1)

            def attention_c(J, j):
                act.wait_ge(s_mix2, J)
                copy(mTh[:, bass.ds(j, 1), :], mix2[:].rearrange("p (a t) -> p a t", a=1), s_mT_h, scale=0.5)

            def head(l, j, next_units):
                J = HEADS * l + j
                first = isinstance(j, int) and j == 0
                never = first and l == 0
                n = MIX[l] + 4 * j
                if not first:
                    attention_a(J)
                next_units(0)
                if not never:
                    act.wait_ge(s_vturn, J)
                    act.wait_ge(s_conv, J)
                act.wait_ge(s_pe, n + 2)
                copy(vb[:], bank[:, 1, :], s_vb)
                if not first:
                    attention_b(J)
                next_units(1)
                act.wait_ge(s_nmax, J + 1)
                for i in range(NT):
                    lo_k, hi_k = (0, P) if i == 0 else (P, 3 * P)
                    for m in range(2):
                        s = scores[:, m, lo_k:hi_k]
                        last = nc.scalar.activation(s, s, ACT.Exp, bias=nmax[:, 2 * i + m:2 * i + m + 1],
                                                    scale=HD ** -0.5, accum_out=ssum[:, 2 * i + m:2 * i + m + 1])
                last.then_inc(s_exp, 1)
                act.wait_ge(s_pe, n + 3)
                copy(c_sb[:], bank[:, 2, 0:T], s_c)
                if not never:
                    act.wait_ge(s_pv, J)
                act.wait_ge(s_vturn, J + 1)
                copy(v_tok[:], bank[:, 6, 0:T], s_v)
                next_units(2)
                if not first:
                    attention_c(J, j - 1)
                if not never:
                    act.wait_ge(s_mix2, J)
                act.wait_ge(s_pe, n + 4)
                nc.scalar.activation(gates_t[:], bank[:, 3, :], ACT.Tanh, scale=0.5).then_inc(s_gates, 1)
                next_units(3)

            def mixer(l):
                head(l, 0, lambda u: split_unit(MIX[l] + 4 + u, MIX[l] + u + 1))
                base = [unit_info(MIX[l] + 4 + u)[2] for u in range(4)]

                def loop(j):
                    def nxt(u):
                        slot = RAW_FIRST[MIX[l]] + u
                        split(slot, u, base[u] + 32 * j, MIX[l] + 4 * j + u + 1)
                    head(l, j, nxt)
                with act.Fori(1, HEADS - 1) as j:
                    loop(j)
                head(l, HEADS - 1, lambda u: split_unit(OUT[l] + u, MIX[l] + 4 * (HEADS - 1) + u + 1))
                J, n = HEADS * (l + 1), OUT[l] + OUT_UNITS
                attention_a(J)
                attention_b(J)
                split_unit(n, OUT[l] + 1)
                attention_c(J, HEADS - 1)
                for m in (1, 2):
                    split_unit(n + m, OUT[l] + m + 1)

            def ffn_silu(i, n):
                if not (isinstance(i, int) and i == 0):
                    act.wait_ge(s_fhid, i)
                act.wait_ge(s_pe, n + 1)
                nc.scalar.activation(silu_g[:], bank[:, 4, :], ACT.Silu).then_inc(s_fsilu, 1)

            def ffn_hT(i):
                act.wait_ge(s_fhid, i + 1)
                copy(hT_h[:], hid[:], s_fhT_h)

            def ffn():
                n = FFN0
                split_unit(n + 3, n + 1)
                ffn_silu(0, n)
                split_unit(n + 4, n + 2)
                ffn_hT(0)
                for i in (1, 2):
                    n = FFN0 + 3 * i - 1
                    split_unit(n + 3, n + 1)
                    ffn_silu(i, n)
                    split_unit(n + 4, n + 2)
                    split_unit(n + 5, n + 3)
                    ffn_hT(i)
                counts = [unit_info(FFN0 + 8 + m + 3)[2] for m in range(6)]
                with act.Fori(0, (PAIRS - 3) // 2 - 1) as r:
                    for m in range(6):
                        i = 3 + m // 3 + 2 * r
                        n = FFN0 + 8 + m
                        slot, part, _ = unit_info(n + 3)
                        split(slot, part, counts[m] + 16 * r, n + 1 + 6 * r)
                        if m % 3 == 0:
                            ffn_silu(i, n + 6 * r)
                        if m % 3 == 2:
                            ffn_hT(i)
                for i in (PAIRS - 2, PAIRS - 1):
                    n = FFN0 + 3 * i - 1
                    split_unit(n + 3, n + 1)
                    ffn_silu(i, n)
                    if n + 4 < FFN0 + FFN_UNITS:
                        split_unit(n + 4, n + 2)
                        split_unit(n + 5, n + 3)
                    else:
                        split_unit(MIX1, FFN0 + 31)
                        act.wait_ge(s_pe, FFN0 + 32)
                    ffn_hT(i)
                split_unit(MIX1 + 1, FFN0 + 32)

            def gathered(E, used):
                if used is not None:
                    act.wait_ge(s_pe, used)
                for b in range(2):
                    act.wait_ge(s_gather, 2 * E + b + 1)
                    copy(xT_h[:, b * CHUNK:(b + 1) * CHUNK], bank[:, 5 + b, :], s_xg_h)

            def experts(pas):
                base = [unit_info(MOE[pas] + 3 + m)[2] for m in range(RAW)]

                def chunk(e, c, units=6, splits=6, gather_next=False):
                    E = EXPERTS * pas + e
                    C = CHUNKS_E * E + c
                    whole = units == 6
                    n = MOE[pas] + EXP_UNITS * e + 6 * c - 2 if whole else MOE[pas]
                    for m in range(units):
                        i = m + 4 if whole else m
                        if m == 3 and gather_next:
                            gathered(E + 1, n + 4)
                        if m < splits:
                            rounds = CHUNKS_E * e + c - 1 + i // 6 if whole else 0
                            split((5 + i + 3) % RAW, i % 3, base[i % 6] + 16 * rounds, n + m + 1)
                        if m == 1:
                            if not (isinstance(C, int) and C == 0):
                                act.wait_ge(s_ehid, C)
                            nc.scalar.activation(silu_g[:], bank[:, 2, :], ACT.Silu).then_inc(s_esilu, 1)
                    act.wait_ge(s_ehturn, C + 1)
                    copy(hT_h[:], bank[:, 4, :], s_ehT_h)

                def output(E, n):
                    if not (isinstance(E, int) and E == 0):
                        act.wait_ge(s_scatter, NT * E)
                    for b in range(2):
                        if b == 0:
                            act.wait_ge(s_half, E + 1)
                        else:
                            act.wait_ge(s_pe, n)
                        copy(eo_h[:, b * CHUNK:(b + 1) * CHUNK], bank[:, b, :], s_eo_h)

                def turned_pick(E):
                    act.wait_ge(s_pickturn, E + 1)
                    copy(pickT[:], bank[:, 7, 0:T], s_pickT)

                gathered(EXPERTS * pas, None)
                chunk(0, 0, units=4, splits=4)
                chunk(0, 1)
                with act.Fori(0, EXPERTS - 1) as e:
                    E = EXPERTS * pas + e
                    with act.Fori(2, CHUNKS_E - 1) as c:
                        chunk(e, c)
                    chunk(e, CHUNKS_E - 1, gather_next=True)
                    chunk(e + 1, 0)
                    output(E, MOE[pas] + EXP_UNITS * (e + 1) + 4)
                    turned_pick(E)
                    chunk(e + 1, 1)
                e = EXPERTS - 1
                with act.Fori(2, CHUNKS_E - 1) as c:
                    chunk(e, c)
                chunk(e, CHUNKS_E - 1, splits=5)
                turned_pick(EXPERTS * pas + e)
                output(EXPERTS * pas + e, MOE[pas] + EXP_UNITS * EXPERTS)

            norm(0, lambda: split_unit(0, None))
            split_unit(1, None)
            split_unit(2, None)
            split_unit(3, None)
            act.wait_ge(s_setup, 2)
            nc.scalar.activation(lame[:], lams[:], ACT.Exp).then_inc(s_setup_a, 1)
            mixer(0)
            norm(1)
            ffn()
            norm(2)
            split_unit(MIX1 + 2, FFN0 + 33)
            split_unit(MIX1 + 3, FFN0 + 33)
            mixer(1)
            copy(rw_h[:], rw[:], s_rw_h)
            norm(3)
            act.wait_ge(s_route, 7)
            nc.scalar.activation(v2e[:], v2[:], ACT.Exp).then_inc(s_v2e, 1)
            nc.scalar.activation(warm[:], v2[:], ACT.Silu)
            experts(0)
            act.wait_ge(s_most, 2)
            with act.If(act.value_load(most_i[0:1, 0:1], min_val=0, max_val=T) > SLOTS):
                for n in range(3):
                    split_unit(MOE2 + n, MOE2)
                experts(1)
                act.wait_ge(s_combined, 2 * EXPERTS)
            norm(4)

        @block.vector
        def _(dve):
            v = nc.vector
            steps = [0]

            def step(ins):
                ins.then_inc(s_setup, 1)
                steps[0] += 1
                dve.wait_ge(s_setup, steps[0])

            def split(n, slot, part):
                dve.wait_ge(s_hi, n + 1)
                v.tensor_tensor(lo[:, part, :], raw[:, slot, :], hi[:, part, :].bitcast(F32),
                                ALU.subtract).then_inc(s_lo, 1)

            def split_unit(n):
                slot, part, _ = unit_info(n)
                split(n, slot, part)

            def norm(q, between=None):
                dve.wait_ge(s_gain, 16 * (q + 1))
                if q == 0:
                    for t in range(NT):
                        dve.wait_ge(s_x[t], 16)
                for t in range(NT):
                    dve.wait_ge(s_rstd, NT * q + t + 1)
                    v.scalar_tensor_tensor(out=normed_x[:, t, :], in0=xres[:, t, :], scalar=rstd[:, t:t + 1],
                                           in1=gain[:], op0=ALU.mult, op1=ALU.mult).then_inc(s_normed, 1)
                if q == 4:
                    return
                for b in range(4):
                    t, half = b // 2, b % 2
                    if b == 2 and between is not None:
                        between()
                    dve.wait_ge(s_xt_h, 4 * q + b + 1)
                    dst = xTl[:, 4 * half:4 * half + 4, t * P:(t + 1) * P]
                    top = xTh[:, 4 * half:4 * half + 4, t * P:(t + 1) * P].bitcast(F32)
                    v.tensor_tensor(dst, bank[:, 4 + b, :].rearrange("p (k t) -> p k t", k=4), top,
                                    ALU.subtract).then_inc(s_xt, 1)
                if q == 3:
                    for t in range(NT):
                        dve.wait_ge(s_nx_h, t + 1)
                        v.tensor_tensor(nxl[:, t, :], normed_x[:, t, :], nxh[:, t, :].bitcast(F32),
                                        ALU.subtract).then_inc(s_nx, 1)

            def rope(J, n):
                dve.wait_ge(s_pe, n + 1)
                if not (isinstance(J, int) and J == 0):
                    dve.wait_ge(s_scores, J)
                both = bank[:, 0, :].rearrange("p (s t) -> p s t", s=2)
                sines, cosines = (cst[:, c:c + T].unsqueeze(1).to_broadcast([P, 2, T]) for c in (C_SIN, C_COS))
                rs, rc = (b[:].rearrange("p (s t) -> p s t", s=2) for b in (rope_s, rope_c))
                for q in range(4):
                    src, dst = slice(32 * q, 32 * q + 32), slice(32 * (q ^ 1), 32 * (q ^ 1) + 32)
                    v.tensor_tensor(rs[dst], both[src], sines[src], ALU.mult)
                v.tensor_tensor(rc, both, cosines, ALU.mult).then_inc(s_rope1, 1)
                dve.wait_ge(s_rope1, J + 1)
                v.tensor_tensor(qkT[:], rope_s[:], rope_c[:], ALU.add).then_inc(s_roped, 1)

            def attention_b(J):
                dve.wait_ge(s_orstd, J)
                for t in range(NT):
                    last = v.tensor_scalar(onorm[:, t * P:(t + 1) * P], bank[:, 7, t * P:(t + 1) * P],
                                           orstd[:, t:t + 1], None, ALU.mult)
                last.then_inc(s_onorm, 1)

            def attention_c1(l, J):
                dve.wait_ge(s_oturn, J)
                dve.wait_ge(s_gates, J)
                v.scalar_tensor_tensor(out=agated[:], in0=gates_t[:, 0:T], scalar=1.0, in1=bank[:, 7, T:2 * T],
                                       op0=ALU.add, op1=ALU.mult).then_inc(s_agated, 1)
                dve.wait_ge(s_agated, J)
                dve.wait_ge(s_cgated, J)
                v.scalar_tensor_tensor(out=mix2[:], in0=agated[:], scalar=sublng[:, l:l + 1], in1=cgated[:],
                                       op0=ALU.mult, op1=ALU.add).then_inc(s_mix2, 1)

            def attention_c2(J, j):
                dve.wait_ge(s_mT_h, J)
                v.scalar_tensor_tensor(out=mTl[:, bass.ds(j, 1), :], in0=mix2[:].rearrange("p (a t) -> p a t", a=1),
                                       scalar=0.5, in1=mTh[:, bass.ds(j, 1), :].bitcast(F32),
                                       op0=ALU.mult, op1=ALU.subtract).then_inc(s_mT, 1)

            def softmax_max(J):
                dve.wait_ge(s_scores, J + 1)
                for m in range(2):
                    last = v.tensor_tensor(scores[:, m, :], bank[:, 4 + m, 0:3 * P], cst[:, C_MASK:C_MASK + 3 * P], ALU.add)
                last.then_inc(s_masked, 1)
                dve.wait_ge(s_masked, J + 1)
                v.tensor_reduce(smax[:, 0:2], scores[:, :, 0:P], AX_X, ALU.max)
                v.tensor_reduce(smax[:, 2:4], scores[:, :, P:3 * P], AX_X, ALU.max).then_inc(s_maxed, 1)
                dve.wait_ge(s_maxed, J + 1)
                v.tensor_scalar(nmax[:], smax[:], -HD ** -0.5, None, ALU.mult).then_inc(s_nmax, 1)

            def short_conv(l, J, j):
                dve.wait_ge(s_c, J + 1)
                v.tensor_tensor(cu[:, TAPS - 1:], bank[:, 2, T:2 * T], c_sb[:], ALU.mult).then_inc(s_cu, 1)
                dve.wait_ge(s_cu, J + 1)
                tap = [colp[:, bass.ds(TAPS * (KD * l + j) + i, 1)] for i in range(TAPS)]
                v.tensor_scalar(conv[:], cu[:, 0:T], tap[0], None, ALU.mult).then_inc(s_tap, 1)
                for i in range(1, TAPS):
                    dve.wait_ge(s_tap, TAPS * J + i)
                    v.scalar_tensor_tensor(out=conv[:], in0=cu[:, i:i + T], scalar=tap[i], in1=conv[:],
                                           op0=ALU.mult, op1=ALU.add).then_inc(s_tap, 1)
                dve.wait_ge(s_tap, TAPS * (J + 1))
                dve.wait_ge(s_vb, J + 1)
                v.tensor_tensor(yconv[:], conv[:], vb[:, T:2 * T], ALU.mult).then_inc(s_conv, 1)

            def gate_conv(J):
                dve.wait_ge(s_gates, J + 1)
                dve.wait_ge(s_conv, J + 1)
                v.scalar_tensor_tensor(out=cgated[:], in0=gates_t[:, T:2 * T], scalar=1.0, in1=yconv[:],
                                       op0=ALU.add, op1=ALU.mult).then_inc(s_cgated, 1)

            def prob_diff(l, J):
                dve.wait_ge(s_exp, J + 1)
                v.reciprocal(srec[:], ssum[:]).then_inc(s_srec, 1)
                dve.wait_ge(s_srec, J + 1)
                v.tensor_scalar(srec1[:], srec[:].rearrange("p (i m) -> p i m", m=2)[:, :, 1], neglam[:, l:l + 1],
                                None, ALU.mult).then_inc(s_srec1, 1)
                dve.wait_ge(s_srec1, J + 1)
                spans = [(0, P), (P, 3 * P)]
                for i, (a, b) in enumerate(spans):
                    last = v.tensor_scalar(pm1[:, a:b], scores[:, 1, a:b], srec1[:, i:i + 1], None, ALU.mult)
                last.then_inc(s_pm1, 1)
                dve.wait_ge(s_pm1, J + 1)
                for i, (a, b) in enumerate(spans):
                    last = v.scalar_tensor_tensor(out=pdiff[:, a:b], in0=scores[:, 0, a:b],
                                                  scalar=srec[:, 2 * i:2 * i + 1], in1=pm1[:, a:b],
                                                  op0=ALU.mult, op1=ALU.add)
                last.then_inc(s_pdiff, 1)

            def parameters():
                step(v.tensor_tensor(lamp, lamv[:, 0::2, :, :], lamv[:, 1::2, :, :], ALU.mult))
                step(v.tensor_reduce(lams[:], lamp, AX_X, ALU.add))
                for l in range(LAYERS):
                    v.tensor_scalar(sublng[:, l:l + 1], colp[:, LAYERS * KD * TAPS + l:LAYERS * KD * TAPS + l + 1],
                                    1.0 - lambda_init(l), None, ALU.mult)
                dve.wait_ge(s_setup_a, 1)
                step(v.tensor_tensor(lamd[:], lame[:, 1, :], lame[:, 0, :], ALU.subtract))
                for l in range(LAYERS):
                    last = v.tensor_scalar(neglam[:, l:l + 1], lamd[:, l:l + 1], -lambda_init(l), None, ALU.add)
                step(last)

            def head(l, j, next_units):
                J = HEADS * l + j
                first = isinstance(j, int) and j == 0
                n = MIX[l] + 4 * j
                if first and l == 0:
                    dve.wait_ge(s_small, 4 * 16)
                rope(J, n)
                if first and l == 0:
                    parameters()
                    split_unit(3)
                next_units(0)
                softmax_max(J)
                next_units(1)
                if not first:
                    attention_b(J)
                short_conv(l, J, j)
                if not first:
                    attention_c1(l, J)
                next_units(2)
                if not first:
                    attention_c2(J, j - 1)
                prob_diff(l, J)
                gate_conv(J)
                next_units(3)

            def mixer(l):
                head(l, 0, lambda u: split_unit(MIX[l] + 4 + u))
                with dve.Fori(1, HEADS - 1) as j:
                    head(l, j, lambda u: split(MIX[l] + 4 * j + 4 + u, RAW_FIRST[MIX[l]] + u, u))
                head(l, HEADS - 1, lambda u: split_unit(OUT[l] + u))
                J, n = HEADS * (l + 1), OUT[l] + OUT_UNITS
                attention_b(J)
                split_unit(n)
                attention_c1(l, J)
                attention_c2(J, HEADS - 1)
                for m in (1, 2):
                    split_unit(n + m)

            def residual(r, unit):
                for t in range(NT):
                    for half in range(2):
                        if (t, half) == (0, 0):
                            dve.wait_ge(s_out, 2 * r + 1)
                        if (t, half) == (1, 0):
                            dve.wait_ge(s_out, 2 * r + 2)
                        if (t, half) == (1, 1):
                            dve.wait_ge(s_pe, unit + 1)
                        part = xres[:, t, half * CHUNK:(half + 1) * CHUNK]
                        last = v.tensor_tensor(part, bank[:, 2 * t + half, :], part, ALU.add)
                    last.then_inc(s_xres, 1)

            def ffn_hid(i, n):
                if not (isinstance(i, int) and i == 0):
                    dve.wait_ge(s_fhT, i)
                dve.wait_ge(s_fsilu, i + 1)
                dve.wait_ge(s_pe, n + 1)
                v.tensor_tensor(hid[:], bank[:, 5, :], silu_g[:], ALU.mult).then_inc(s_fhid, 1)

            def ffn_hT(i):
                dve.wait_ge(s_fhT_h, i + 1)
                v.tensor_tensor(hT_l[:], hid[:], hT_h[:].bitcast(F32), ALU.subtract).then_inc(s_fhT, 1)

            def ffn():
                split_unit(FFN0 + 3)
                split_unit(FFN0 + 4)
                ffn_hid(0, FFN0 + 1)
                ffn_hT(0)
                for i in (1, 2):
                    n = FFN0 + 3 * i - 1
                    split_unit(n + 3)
                    ffn_hid(i, n + 1)
                    split_unit(n + 4)
                    split_unit(n + 5)
                    ffn_hT(i)
                with dve.Fori(0, (PAIRS - 3) // 2 - 1) as r:
                    for m in range(6):
                        i = 3 + m // 3 + 2 * r
                        n = FFN0 + 8 + m
                        slot, part, _ = unit_info(n + 3)
                        if m % 3 == 1:
                            ffn_hid(i, n + 6 * r)
                        split(n + 3 + 6 * r, slot, part)
                        if m % 3 == 2:
                            ffn_hT(i)
                for i in (PAIRS - 2, PAIRS - 1):
                    n = FFN0 + 3 * i - 1
                    split_unit(n + 3)
                    ffn_hid(i, n + 1)
                    split_unit(n + 4 if i == PAIRS - 2 else MIX1)
                    if i == PAIRS - 2:
                        split_unit(n + 5)
                    ffn_hT(i)
                split_unit(MIX1 + 1)

            def route():
                dve.wait_ge(s_rw_h, 1)
                v.tensor_tensor(rw_l[:], rw[:], rw_h[:].bitcast(F32), ALU.subtract).then_inc(s_rw, 1)

            r_steps = [0]

            def rstep(ins):
                ins.then_inc(s_route, 1)
                r_steps[0] += 1
                dve.wait_ge(s_route, r_steps[0])

            def top_two():
                dve.wait_ge(s_logit, 1)
                rstep(v.tensor_copy(logitT[0:EXPERTS, :], bank[0:EXPERTS, 0, 0:T]))
                dve.wait_ge(s_logit, 2)
                rstep(v.tensor_copy(logit[:], bank[:, 2, 0:NT * EXPERTS].rearrange("p (t e) -> p t e", t=NT)))
                mine = logit[:].unsqueeze(3).to_broadcast([P, NT, EXPERTS, EXPERTS])
                other = logit[:].unsqueeze(2).to_broadcast([P, NT, EXPERTS, EXPERTS])
                tri = cst[:, C_TRI:C_TRI + EXPERTS * EXPERTS].rearrange("p (e j) -> p e j", e=EXPERTS)
                v.tensor_tensor(above, other, mine, ALU.is_gt)
                rstep(v.tensor_tensor(ties, other, mine, ALU.is_equal))
                for t in range(NT):
                    last = v.tensor_tensor(ties[:, t], ties[:, t], tri, ALU.mult)
                rstep(last)
                rstep(v.tensor_tensor(above, above, ties, ALU.add))
                v.tensor_reduce(rank[:], above, AX_X, ALU.add)
                rstep(v.tensor_reduce(v1[:], logit[:], AX_X, ALU.max))
                v.tensor_scalar(top1[:], rank[:], 0.0, None, ALU.is_equal)
                v.tensor_scalar(chosen[:], rank[:], 2.0, None, ALU.is_lt)
                v.tensor_scalar(top2[:], rank[:], 1.0, None, ALU.is_equal).then_inc(s_chosen, 1)
                dve.wait_ge(s_chosen, 1)
                v.tensor_tensor(ties[:, :, 0, :], top2[:], logit[:], ALU.mult).then_inc(s_chosen, 1)
                dve.wait_ge(s_chosen, 2)
                v.tensor_reduce(w2[:], ties[:, :, 0, :], AX_X, ALU.add).then_inc(s_chosen, 1)
                dve.wait_ge(s_chosen, 3)
                rstep(v.tensor_tensor(v2[:], w2[:], v1[:], ALU.subtract))
                dve.wait_ge(s_count, 1)
                rstep(v.tensor_scalar(place[:], bank[:, 1, 0:NT * EXPERTS].rearrange("p (t e) -> p t e", t=NT),
                                      1.0, None, ALU.add))
                rstep(v.tensor_tensor(place[:], place[:], chosen[:], ALU.mult))
                rstep(v.tensor_scalar(place[:], place[:], -1.0, None, ALU.add))

            def route_weights():
                dve.wait_ge(s_v2e, 1)
                rstep(v.tensor_scalar(den[:], v2e[:], 1.0, None, ALU.add))
                rstep(v.reciprocal(w1[:], den[:]))
                rstep(v.tensor_tensor(w2[:], w1[:], v2e[:], ALU.mult))
                for t in range(NT):
                    last = v.tensor_scalar(egate[:, t, :], top1[:, t, :], w1[:, t:t + 1], None, ALU.mult)
                rstep(last)
                for t in range(NT):
                    last = v.scalar_tensor_tensor(out=egate[:, t, :], in0=top2[:, t, :], scalar=w2[:, t:t + 1],
                                                  in1=egate[:, t, :], op0=ALU.mult, op1=ALU.add)
                rstep(last)
                v.tensor_reduce(most[:], bank[:, 1, NT * EXPERTS:(NT + 1) * EXPERTS], AX_X, ALU.max).then_inc(s_most, 1)
                dve.wait_ge(s_most, 1)
                v.tensor_copy(most_i[:], most[:]).then_inc(s_most, 1)

            def pick_for(dst, E, e, s):
                for t in range(NT):
                    last = v.tensor_scalar(dst[:, t, :], cst[:, C_IOTA:C_IOTA + SLOTS],
                                           place[:, t, bass.ds(e, 1)], None, ALU.is_equal)
                last.then_inc(s, 1)

            def gathered(E):
                for b in range(2):
                    dve.wait_ge(s_xg_h, 2 * E + b + 1)
                    part = slice(b * CHUNK, (b + 1) * CHUNK)
                    v.tensor_tensor(xT_l[:, part], bank[:, 5 + b, :], xT_h[:, part].bitcast(F32),
                                    ALU.subtract).then_inc(s_xg, 1)

            def combine(E, e, final=False):
                for b in range(4):
                    t, half = b // 2, b % 2
                    if half == 0:
                        dve.wait_ge(s_scatter, NT * E + t + 1)
                    part = xres[:, t, half * CHUNK:(half + 1) * CHUNK]
                    last = v.scalar_tensor_tensor(out=part, in0=bank[:, (5, 6, 7, 4)[b], :],
                                                  scalar=egate[:, t, bass.ds(e, 1)], in1=part,
                                                  op0=ALU.mult, op1=ALU.add)
                    if final and half == 1:
                        last.then_inc(s_xres, 1)
                if final:
                    last = v.memset(mark[:], 0.0)
                last.then_inc(s_combined, 1)

            def output(E):
                for b in range(2):
                    dve.wait_ge(s_eo_h, 2 * E + b + 1)
                    part = slice(b * CHUNK, (b + 1) * CHUNK)
                    v.tensor_tensor(eo_l[:, part], bank[:, b, :], eo_h[:, part].bitcast(F32),
                                    ALU.subtract).then_inc(s_eo, 1)

            def pick_to_scatter(E, e):
                if not (isinstance(E, int) and E == 0):
                    dve.wait_ge(s_pickturn, E)
                pick_for(pick_s, E, e, s_pick_s)

            def hidden_low(C):
                dve.wait_ge(s_ehT_h, C + 1)
                v.tensor_tensor(hT_l[:], bank[:, 4, :], hT_h[:].bitcast(F32), ALU.subtract).then_inc(s_ehT, 1)

            def experts(pas):
                def chunk(e, c, units=6, splits=6, gather_next=False, combines=False):
                    E = EXPERTS * pas + e
                    C = CHUNKS_E * E + c
                    whole = units == 6
                    n = MOE[pas] + EXP_UNITS * e + 6 * c - 2 if whole else MOE[pas]
                    for m in range(units):
                        i = m + 4 if whole else m
                        if m == 3 and gather_next:
                            gathered(E + 1)
                        if m == 3:
                            dve.wait_ge(s_esilu, C + 1)
                            dve.wait_ge(s_pe, n + 4)
                            v.tensor_tensor(hid[:], bank[:, 3, :], silu_g[:], ALU.mult).then_inc(s_ehid, 1)
                        if m == 4 and splits == 5:
                            hidden_low(C)
                        if m < splits:
                            split(n + m + 3, (5 + i + 3) % RAW, i % 3)
                        if m == 3 and combines:
                            combine(E - 1, e - 1)
                    if splits != 5:
                        hidden_low(C)

                E0 = EXPERTS * pas
                if pas:
                    dve.wait_ge(s_gather, 2 * E0)
                pick_for(pick, E0, 0, s_pick)
                if not pas:
                    route_weights()
                gathered(E0)
                chunk(0, 0, units=4, splits=4)
                chunk(0, 1)
                with dve.Fori(0, EXPERTS - 1) as e:
                    E = E0 + e
                    with dve.Fori(2, CHUNKS_E - 1) as c:
                        chunk(e, c)
                    dve.wait_ge(s_gather, 2 * (E + 1))
                    pick_for(pick, E + 1, e + 1, s_pick)
                    chunk(e, CHUNKS_E - 1, gather_next=True)
                    pick_to_scatter(E, e)
                    chunk(e + 1, 0)
                    output(E)
                    chunk(e + 1, 1, combines=True)
                e = EXPERTS - 1
                with dve.Fori(2, CHUNKS_E - 1) as c:
                    chunk(e, c)
                pick_to_scatter(E0 + e, e)
                chunk(e, CHUNKS_E - 1, splits=5)
                output(E0 + e)
                combine(E0 + e, e, final=True)

            v.memset(cu[:], 0.0)
            v.memset(rw[:, KD * EXPERTS:], 0.0)
            norm(0, lambda: split_unit(0))
            split_unit(1)
            split_unit(2)
            mixer(0)
            residual(0, OUT0 + OUT_UNITS - 1)
            norm(1)
            ffn()
            residual(1, FFN0 + FFN_UNITS - 1)
            norm(2)
            split_unit(MIX1 + 2)
            split_unit(MIX1 + 3)
            mixer(1)
            route()
            residual(2, OUT1 + OUT_UNITS - 1)
            norm(3)
            top_two()
            experts(0)
            with dve.If(dve.value_load(most_i[0:1, 0:1], min_val=0, max_val=T) > SLOTS):
                for n in range(3):
                    split_unit(MOE2 + n)
                v.tensor_scalar(place[:], place[:], -float(SLOTS), None, ALU.add).then_inc(s_most, 1)
                dve.wait_ge(s_most, 3)
                experts(1)
            norm(4)

        @block.gpsimd
        def _(pool):
            def inv_root(src, mean, dst, per, s_mean, s_out, value):
                w = src.shape[1]
                nc.gpsimd.tensor_tensor(mean, src, cst[:, per:per + w], ALU.mult).then_inc(s_mean, 1)
                pool.wait_ge(s_mean, 2 * value - 1)
                nc.gpsimd.tensor_tensor(mean, mean, cst[:, C_EPS:C_EPS + w], ALU.add).then_inc(s_mean, 1)
                pool.wait_ge(s_mean, 2 * value)
                nc.gpsimd.tensor_tensor(dst, mean, cst[:, C_NH:C_NH + w], ALU.pow).then_inc(s_out, 1)

            def norm(q):
                for t in range(NT):
                    one = slice(t, t + 1)
                    pool.wait_ge(s_ss, NT * q + t + 1)
                    inv_root(ss[:, one], ms[:, one], rstd[:, one], C_PER_D, s_ms, s_rstd, NT * q + t + 1)

            pool.wait_ge(s_const, 16)
            norm(0)
            for l in range(LAYERS):
                with pool.Fori(HEADS * l + 1, HEADS * l + HEADS + 1) as J:
                    pool.wait_ge(s_osq, J)
                    inv_root(osq[:], oms[:], orstd[:], C_PER_VD, s_oms, s_orstd, J)
                norm(2 * l + 1)
                if l == 0:
                    norm(2)
            norm(4)

        @block.tensor
        def _(pe):
            def mm(o, lhsT, rhs, start, stop):
                return nc.tensor.matmul(o, lhsT, rhs, start=start, stop=stop)

            def mm3(o, ah, al, bh, bl, start, stop):
                mm(o, ah, bh, start, False)
                mm(o, ah, bl, False, False)
                return mm(o, al, bh, False, stop)

            def keep_clock(b, n):
                for _ in range(n):
                    mm(bank[:, b, 0:T], ident.bitcast(BF16)[:, 0:P], ident.bitcast(BF16), True, True)

            def norm(q):
                keep_clock(7, (14, 34, 20, 34)[q])
                for t in range(NT):
                    if t:
                        keep_clock(7, 5)
                    pe.wait_ge(s_normed, NT * q + t + 1)
                    for half in range(2):
                        for k in range(4):
                            kk = 4 * half + k
                            last = nc.tensor.transpose(bank[:, 4 + 2 * t + half, k * P:(k + 1) * P],
                                                       normed_x[:, t, kk * P:(kk + 1) * P], ident)
                        last.then_inc(s_turned, 1)
                keep_clock(3, 40 if q == 0 else 10)

            def attention_a(J):
                pe.wait_ge(s_pdiff, J)
                pe.wait_ge(s_v, J)
                for i in range(3):
                    last = nc.tensor.transpose(bank[:, 6, i * P:(i + 1) * P], pdiff[:, i * P:(i + 1) * P], ident)
                last.then_inc(s_pturn, 1)

            def attention_b(J):
                pe.wait_ge(s_pT, J)
                if not (isinstance(J, int) and J == 1):
                    pe.wait_ge(s_mix2, J - 1)
                mm(bank[:, 7, 0:P], pT[:, 0:P], v_tok[:, 0:P], True, True)
                mm(bank[:, 7, P:2 * P], pT[:, P:2 * P], v_tok[:, 0:P], True, False)
                mm(bank[:, 7, P:2 * P], pT[:, 2 * P:3 * P], v_tok[:, P:2 * P], False, True).then_inc(s_pv, 1)

            def attention_c(J):
                pe.wait_ge(s_onorm, J)
                for t in range(NT):
                    last = nc.tensor.transpose(bank[:, 7, T + t * P:T + (t + 1) * P], onorm[:, t * P:(t + 1) * P], ident)
                last.then_inc(s_oturn, 1)

            def turn_v(J):
                pe.wait_ge(s_vb, J + 1)
                if not (isinstance(J, int) and J == 0):
                    pe.wait_ge(s_pT, J)
                for t in range(NT):
                    last = nc.tensor.transpose(bank[:, 6, t * P:(t + 1) * P], vb[:, t * P:(t + 1) * P], ident)
                last.then_inc(s_vturn, 1)

            def qk_scores(J):
                pe.wait_ge(s_roped, J + 1)
                if not (isinstance(J, int) and J == 0):
                    pe.wait_ge(s_nmax, J)
                for m in range(2):
                    rows = slice(HD * m, HD * (m + 1))
                    mm(bank[:, 4 + m, 0:P], qkT[rows, 0:P], qkT[rows, T:T + P], True, True)
                    last = mm(bank[:, 4 + m, P:3 * P], qkT[rows, P:2 * P], qkT[rows, T:2 * T], True, True)
                last.then_inc(s_scores, 1)

            def stream_half(q, k):
                if q is not None and k in (0, KD // 2):
                    pe.wait_ge(s_xt, 4 * q + (3 if k == 0 else 4))

            def projection(b, off, u, s, fresh=None):
                wh, wl = block_of(hi, u, s=2, k=KD), block_of(lo, u, s=2, k=KD)
                for k in range(KD):
                    stream_half(fresh, k)
                    last = mm3(bank[:, b, off:off + T], wh[:, s, k, :], wl[:, s, k, :], xTh[:, k, :], xTl[:, k, :],
                               k == 0, k == KD - 1)
                return last

            def head(l, j):
                J = HEADS * l + j
                first = isinstance(j, int) and j == 0
                never = first and l == 0
                n = MIX[l] + 4 * j
                pe.wait_ge(s_lo, n + 1)
                if not never:
                    pe.wait_ge(s_roped, J)
                projection(0, 0, 0, 0, 2 * l if first else None)
                projection(0, T, 0, 1).then_inc(s_pe, 1)
                if not first:
                    attention_a(J)
                pe.wait_ge(s_lo, n + 2)
                if not never:
                    pe.wait_ge(s_vb, J)
                projection(1, 0, 1, 0)
                projection(1, T, 1, 1).then_inc(s_pe, 1)
                if not first:
                    attention_b(J)
                qk_scores(J)
                pe.wait_ge(s_lo, n + 3)
                if not never:
                    pe.wait_ge(s_conv, J)
                projection(2, 0, 2, 0)
                projection(2, T, 2, 1).then_inc(s_pe, 1)
                turn_v(J)
                if not first:
                    attention_c(J)
                pe.wait_ge(s_lo, n + 4)
                if not never:
                    pe.wait_ge(s_gates, J)
                projection(3, 0, 3, 0)
                projection(3, T, 3, 1).then_inc(s_pe, 1)

            def out_unit(l, u):
                pe.wait_ge(s_lo, OUT[l] + u + 1)
                pe.wait_ge(s_mT, HEADS * l + 2 * u + 2)
                wh, wl = block_of(hi, u, k=2), block_of(lo, u, k=2)
                for b in range(4):
                    if u == 0 and b == 3:
                        pe.wait_ge(s_gates, HEADS * (l + 1))
                    for kk in range(2):
                        k = 2 * u + kk
                        tok, ch = slice((b // 2) * P, (b // 2 + 1) * P), slice((b % 2) * CHUNK, (b % 2 + 1) * CHUNK)
                        last = mm3(bank[:, b, :], mTh[:, k, tok], mTl[:, k, tok], wh[:, kk, ch], wl[:, kk, ch],
                                   k == 0, k == KD - 1)
                    if u == OUT_UNITS - 1 and b in (1, 2):
                        last.then_inc(s_out, 1)
                last.then_inc(s_pe, 1)

            def mixer(l):
                head(l, 0)
                if l == 0:
                    head(l, 1)
                with pe.Fori(2 if l == 0 else 1, HEADS) as j:
                    head(l, j)
                J = HEADS * (l + 1)
                attention_a(J)
                pe.wait_ge(s_conv, J)
                out_unit(l, 0)
                attention_b(J)
                out_unit(l, 1)
                attention_c(J)
                out_unit(l, 2)
                out_unit(l, 3)

            def ffn_cols(b, part, fresh=None):
                wh, wl = block_of(hi, part, k=KD), block_of(lo, part, k=KD)
                for f in range(2):
                    for k in range(KD):
                        if f == 0:
                            stream_half(fresh, k)
                        cols_f = slice(f * P, (f + 1) * P)
                        last = mm3(bank[:, b, f * T:(f + 1) * T], wh[:, k, cols_f], wl[:, k, cols_f],
                                   xTh[:, k, :], xTl[:, k, :], k == 0, k == KD - 1)
                last.then_inc(s_pe, 1)

            def ffn_down(i, n, part, first, final):
                pe.wait_ge(s_lo, n + 1)
                pe.wait_ge(s_fhT, i + 1)
                wh, wl = block_of(hi, part, r=2), block_of(lo, part, r=2)
                for b in range(4):
                    for f in range(2):
                        tok = slice(f * T + (b // 2) * P, f * T + (b // 2 + 1) * P)
                        ch = slice((b % 2) * CHUNK, (b % 2 + 1) * CHUNK)
                        last = mm3(bank[:, b, :], hT_h[:, tok], hT_l[:, tok], wh[:, f, ch], wl[:, f, ch],
                                   first and f == 0, final and f == 1)
                    if final and b in (1, 2):
                        last.then_inc(s_out, 1)
                last.then_inc(s_pe, 1)

            def ffn_pair(i, first_down=False):
                n = FFN0 + 3 * i - 1
                pe.wait_ge(s_lo, n + 1)
                pe.wait_ge(s_fsilu, i)
                ffn_cols(4, 2)
                pe.wait_ge(s_lo, n + 2)
                pe.wait_ge(s_fhid, i)
                ffn_cols(5, 0)
                ffn_down(i - 1, n + 2, 1, first_down, False)

            def ffn():
                pe.wait_ge(s_lo, FFN0 + 1)
                ffn_cols(4, 0, 1)
                pe.wait_ge(s_lo, FFN0 + 2)
                ffn_cols(5, 1)
                ffn_pair(1, True)
                with pe.Fori(2, PAIRS) as i:
                    ffn_pair(i)
                ffn_down(PAIRS - 1, FFN0 + FFN_UNITS - 1, (FFN_UNITS - 1) % 3, False, True)

            def route():
                pe.wait_ge(s_small, 4 * 16)
                pe.wait_ge(s_rw, 1)
                for k in range(KD):
                    stream_half(3, k)
                    cols_k = slice(k * EXPERTS, k * EXPERTS + P)
                    last = mm3(bank[:, 0, 0:T], rw_h[:, cols_k], rw_l[:, cols_k], xTh[:, k, :], xTl[:, k, :],
                               k == 0, k == KD - 1)
                last.then_inc(s_logit, 1)
                keep_clock(3, 6)
                pe.wait_ge(s_route, 1)
                for t in range(NT):
                    last = nc.tensor.transpose(bank[:, 2, t * EXPERTS:(t + 1) * EXPERTS],
                                               logitT[0:EXPERTS, t * P:(t + 1) * P], ident[0:EXPERTS, 0:EXPERTS])
                last.then_inc(s_logit, 1)
                keep_clock(3, 18)
                pe.wait_ge(s_chosen, 1)
                upper, ones = cst[:, C_UPPER:C_UPPER + P], cst[:, C_ONES:C_ONES + P]
                E = EXPERTS
                mm(bank[:, 1, 0:E], upper, chosen[:, 0, :], True, True)
                mm(bank[:, 1, E:2 * E], ones, chosen[:, 0, :], True, False)
                mm(bank[:, 1, E:2 * E], upper, chosen[:, 1, :], False, True)
                mm(bank[:, 1, 2 * E:3 * E], ones, chosen[:, 0, :], True, False)
                mm(bank[:, 1, 2 * E:3 * E], ones, chosen[:, 1, :], False, True).then_inc(s_count, 1)
                keep_clock(3, 10)

            def gather(E):
                pe.wait_ge(s_pick, E + 1)
                if not (isinstance(E, int) and E <= 1):
                    pe.wait_ge(s_combined, E - 1)
                for k in range(KD):
                    o = bank[:, 5 + k // 4, (k % 4) * SLOTS:(k % 4 + 1) * SLOTS]
                    d = slice(k * P, (k + 1) * P)
                    for t in range(NT):
                        mm(o, nxh[:, t, d], pick[:, t, :], t == 0, False)
                        last = mm(o, nxl[:, t, d], pick[:, t, :], False, t == NT - 1)
                    if k % 4 == 3:
                        last.then_inc(s_gather, 1)

            def scatter(E):
                pe.wait_ge(s_pickT, E + 1)
                for b in range(4):
                    if b < 2:
                        pe.wait_ge(s_eo, 2 * E + b + 1)
                    o = bank[:, (5, 6, 7, 4)[b], :]
                    tok, ch = slice((b // 2) * P, (b // 2 + 1) * P), slice((b % 2) * CHUNK, (b % 2 + 1) * CHUNK)
                    mm(o, pickT[:, tok], eo_h[:, ch], True, False)
                    last = mm(o, pickT[:, tok], eo_l[:, ch], False, True)
                    if b % 2 == 1:
                        last.then_inc(s_scatter, 1)

            def expert_cols(b, n, at, fresh=None):
                for half in range(2):
                    part = (at + half) % 3
                    pe.wait_ge(s_lo, n + half + 1)
                    wh, wl = block_of(hi, part, k=4), block_of(lo, part, k=4)
                    if fresh is not None:
                        pe.wait_ge(s_xg, 2 * fresh + half + 1)
                    for kk in range(4):
                        k = 4 * half + kk
                        last = mm3(bank[:, b, :], xgh[:, k, :], xgl[:, k, :], wh[:, kk, :], wl[:, kk, :],
                                   k == 0, k == KD - 1)
                    last.then_inc(s_pe, 1)

            def turn_hidden(C):
                pe.wait_ge(s_ehid, C + 1)
                for f in range(4):
                    last = nc.tensor.transpose(bank[:, 4, f * P:(f + 1) * P], hid[:, f * P:(f + 1) * P], ident)
                last.then_inc(s_ehturn, 1)

            def expert_down(C, n, at, first, final):
                pe.wait_ge(s_ehT, C + 1)
                for half in range(2):
                    part = (at + half) % 3
                    pe.wait_ge(s_lo, n + half + 1)
                    wh, wl = block_of(hi, part, r=2), block_of(lo, part, r=2)
                    for b in range(2):
                        ch = slice(b * CHUNK, (b + 1) * CHUNK)
                        for r in range(2):
                            f = 2 * half + r
                            rows = slice(f * SLOTS, (f + 1) * SLOTS)
                            last = mm3(bank[:, b, :], hT_h[:, rows], hT_l[:, rows], wh[:, r, ch], wl[:, r, ch],
                                       first and f == 0, final and f == 3)
                        if final and half == 1 and b == 0:
                            last.then_inc(s_half, 1)
                    last.then_inc(s_pe, 1)

            def experts(pas):
                def chunk(e, c, down=True, start_down=False, final_down=False, gather_next=False, scatter_last=False,
                          fresh=None):
                    E = EXPERTS * pas + e
                    C = CHUNKS_E * E + c
                    n = MOE[pas] + EXP_UNITS * e + 6 * c - 2 if down else MOE[pas]
                    at = 4 if down else 0
                    if not (isinstance(C, int) and C == 0):
                        pe.wait_ge(s_esilu, C)
                    expert_cols(2, n, at, fresh)
                    if gather_next:
                        gather(E + 1)
                    if not (isinstance(C, int) and C == 0):
                        pe.wait_ge(s_ehid, C)
                    expert_cols(3, n + 2, at + 2)
                    if scatter_last:
                        pe.wait_ge(s_ehT, C)
                        scatter(E - 1)
                    if down:
                        if start_down and not (isinstance(E, int) and E == 0):
                            pe.wait_ge(s_eo, 2 * E)
                        expert_down(C - 1, n + 4, at + 4, start_down, final_down)
                    if scatter_last:
                        pe.wait_ge(s_combined, E)
                    turn_hidden(C)

                def turn_pick(E):
                    pe.wait_ge(s_pick_s, E + 1)
                    if not (isinstance(E, int) and E == 0):
                        pe.wait_ge(s_combined, E)
                    for t in range(NT):
                        turned = nc.tensor.transpose(bank[:, 7, t * P:(t + 1) * P], pick_s[:, t, :], ident)
                    turned.then_inc(s_pickturn, 1)

                E0 = EXPERTS * pas
                gather(E0)
                chunk(0, 0, down=False, fresh=E0)
                chunk(0, 1, start_down=True)
                with pe.Fori(0, EXPERTS - 1) as e:
                    E = E0 + e
                    with pe.Fori(2, CHUNKS_E - 1) as c:
                        chunk(e, c)
                    chunk(e, CHUNKS_E - 1, gather_next=True)
                    chunk(e + 1, 0, final_down=True, fresh=E + 1)
                    turn_pick(E)
                    chunk(e + 1, 1, start_down=True, scatter_last=True)
                e = EXPERTS - 1
                with pe.Fori(2, CHUNKS_E - 1) as c:
                    chunk(e, c)
                chunk(e, CHUNKS_E - 1)
                turn_pick(E0 + e)
                expert_down(CHUNKS_E * (E0 + e + 1) - 1, MOE[pas] + EXP_UNITS * EXPERTS - 2, 4, False, True)
                pe.wait_ge(s_ehT, CHUNKS_E * (E0 + e + 1))
                scatter(E0 + e)

            pe.wait_ge(s_const, 16)
            norm(0)
            mixer(0)
            norm(1)
            ffn()
            norm(2)
            mixer(1)
            norm(3)
            route()
            pe.wait_ge(s_nx, NT)
            experts(0)
            pe.wait_ge(s_most, 2)
            with pe.If(pe.value_load(most_i[0:1, 0:1], min_val=0, max_val=T) > SLOTS):
                pe.wait_ge(s_combined, EXPERTS)
                experts(1)


def constants():
    import numpy as np

    f = np.float32
    c = np.zeros((P, C_ALL), f)
    c[:, C_ID:C_ID + P] = np.eye(P, dtype=f)
    inv = (f(1.0) / (f(THETA) ** (np.arange(0, HD, 2, dtype=f) / f(HD)))).astype(f)
    ang = np.arange(T, dtype=f)[None, :] * inv[:, None]
    cos, sin = np.cos(ang).astype(f), np.sin(ang).astype(f)
    for q in range(4):
        rows = slice(32 * q, 32 * q + 32)
        c[rows, C_COS:C_COS + T] = cos
        c[rows, C_SIN:C_SIN + T] = sin if q % 2 == 0 else -sin
    row, col = np.arange(P)[:, None], np.arange(P)[None, :]
    future = np.where(col > row, f(-3e38), f(0))
    c[:, C_MASK:C_MASK + P] = future
    c[:, C_MASK + 2 * P:C_MASK + 3 * P] = future
    c[:, C_UPPER:C_UPPER + P] = (row < col)
    c[:, C_ONES:C_ONES + P] = 1
    c[:, C_IOTA:C_IOTA + SLOTS] = np.arange(SLOTS)
    e = np.arange(EXPERTS)
    c[:, C_TRI:C_TRI + EXPERTS ** 2] = (e[None, :] < e[:, None]).reshape(-1)
    c[:, C_NH:C_NH + NT] = -0.5
    c[:, C_EPS:C_EPS + NT] = EPS
    c[:, C_PER_D:C_PER_D + NT] = 1 / D
    c[:, C_PER_VD:C_PER_VD + NT] = 1 / VD
    return c


def build(nc, arrays):
    ins = {n: nc.dram_tensor(n, a.shape, F32, kind="ExternalInput").ap() for n, a in arrays.items()}
    out = nc.dram_tensor("out", (T, D), F32, kind="ExternalOutput").ap()
    hybrid_trunk(nc, *ins.values(), out)


def layout(i):
    import numpy as np

    c = np.ascontiguousarray
    a = {n: np.asarray(x) for n, x in i.items()}
    taps = a["conv_w"].reshape(LAYERS, TAPS, KD, P).transpose(3, 0, 2, 1).reshape(P, -1)
    return {
        "x": c(a["x"].reshape(T, D)),
        "w_in": c(a["w_in"]),
        "w_out": c(a["w_out"]),
        "gains": c(np.stack([a["norm_mix"][0], a["norm_ffn"][0], a["norm_mix"][1], a["norm_ffn"][1], a["norm_final"]])),
        "lam_rows": c(np.stack([a["lam_q1"], a["lam_k1"], a["lam_q2"], a["lam_k2"]]).reshape(1, -1)),
        "cols": c(np.concatenate([taps, a["subln_g"].T], axis=1)),
        "router": c(a["router_w"][0].reshape(KD, P, EXPERTS).transpose(1, 0, 2).reshape(P, -1)),
        "w_gate": c(a["ffn_w_gate"]),
        "w_up": c(a["ffn_w_up"]),
        "w_down": c(a["ffn_w_down"]),
        "e_gate": c(a["exp_w_gate"]),
        "e_up": c(a["exp_w_up"]),
        "e_down": c(a["exp_w_down"]),
        "consts": constants(),
    }


def kernel(**inputs):
    import concourse.bacc as bacc
    from concourse.bass_utils import run_bass_kernel_spmd

    nc = bacc.Bacc("TRN2", target_bir_lowering=False, num_devices=1)
    arrays = layout(inputs)
    build(nc, arrays)
    r = run_bass_kernel_spmd(nc, [arrays], core_ids=[0])
    return r.results[0]["out"].reshape(1, T, D)
```
